# Optimizing a Trainium2 kernel written in Bass

```python
import math
import jax
import jax.numpy as jnp
from jax import lax
import numpy as np
import jax, jax.numpy as jnp

D_MODEL = 1024
BATCH = 1
SEQ = 256
DEPTH = 2

N_MIXERS = 4
HEAD_DIM = 64
N_HEADS = D_MODEL // HEAD_DIM
ROPE_THETA = 10000.0
RMS_EPS = 1e-6
NEG_INF = -1e30
ATTN_QBLOCK = 128
MOBA_BLOCK = 256
MOBA_TOPK = 3
MOBA_QCHUNK = 32
MLA_HEADS = N_HEADS
MLA_Q_LORA = 3 * D_MODEL // 8
MLA_KV_LORA = D_MODEL // 4
MLA_NOPE = HEAD_DIM
MLA_ROPE = HEAD_DIM // 2
MLA_V = HEAD_DIM
DIL_GROUPS = ((128, 1), (512, 4), (2048, 16))
DIL_HEADS = N_HEADS
DIL_BLOCK = 128
SB_HEADS = N_HEADS
SB_QBLOCK = 128
D_FF = ((8 * D_MODEL // 3 + 255) // 256) * 256
CONV_WIDTH = 3


def rms_norm(x, g):
    xf = x.astype(jnp.float32)
    y = xf * lax.rsqrt(jnp.mean(xf * xf, axis=-1, keepdims=True) + RMS_EPS)
    return (y * g.astype(jnp.float32)).astype(x.dtype)

def rope_tables(pos, dim):
    inv = ROPE_THETA ** (-jnp.arange(0, dim, 2, dtype=jnp.float32) / dim)
    ang = pos[:, None] * inv[None, :]
    return jnp.cos(ang), jnp.sin(ang)

def apply_rope(x, cos, sin):
    half = x.shape[-1] // 2
    x1, x2 = x[..., :half], x[..., half:]
    c = cos[None, :, None, :].astype(x.dtype)
    s = sin[None, :, None, :].astype(x.dtype)
    return jnp.concatenate([x1 * c - x2 * s, x2 * c + x1 * s], axis=-1)

def moba_attention(q, k, v):
    B, S, H, dh = q.shape
    scale = dh ** -0.5
    nb = -(-S // MOBA_BLOCK)
    sp = nb * MOBA_BLOCK
    padw = ((0, 0), (0, sp - S), (0, 0), (0, 0))
    qh = jnp.pad(q, padw).transpose(0, 2, 1, 3)
    kh = jnp.pad(k, padw).transpose(0, 2, 1, 3)
    vh = jnp.pad(v, padw).transpose(0, 2, 1, 3)
    kblk = kh.reshape(B, H, nb, MOBA_BLOCK, dh)
    vblk = vh.reshape(B, H, nb, MOBA_BLOCK, dh)
    kmean = jnp.mean(kblk.astype(jnp.float32), axis=3)
    topk = min(MOBA_TOPK, nb)
    bi = jnp.arange(B)[:, None, None, None]
    hi = jnp.arange(H)[None, :, None, None]
    blk_ids = jnp.arange(nb)

    def step(c):
        start = c * MOBA_QCHUNK
        blk = start // MOBA_BLOCK
        qc = lax.dynamic_slice_in_dim(qh, start, MOBA_QCHUNK, axis=2)
        qpos = start + jnp.arange(MOBA_QCHUNK)
        gate = jnp.einsum("bhqd,bhnd->bhqn", qc.astype(jnp.float32), kmean)
        gate = jnp.where(blk_ids < blk, gate, NEG_INF)
        _, gidx = lax.top_k(gate, topk)
        valid = gidx < blk
        ksel = kblk[bi, hi, gidx]
        vsel = vblk[bi, hi, gidx]
        s_sel = jnp.einsum("bhqd,bhqnkd->bhqnk", qc, ksel, preferred_element_type=jnp.float32) * scale
        s_sel = jnp.where(valid[..., None], s_sel, NEG_INF)
        s_sel = s_sel.reshape(B, H, MOBA_QCHUNK, topk * MOBA_BLOCK)
        kown = lax.dynamic_slice_in_dim(kh, blk * MOBA_BLOCK, MOBA_BLOCK, axis=2)
        vown = lax.dynamic_slice_in_dim(vh, blk * MOBA_BLOCK, MOBA_BLOCK, axis=2)
        s_own = jnp.einsum("bhqd,bhkd->bhqk", qc, kown, preferred_element_type=jnp.float32) * scale
        kpos = blk * MOBA_BLOCK + jnp.arange(MOBA_BLOCK)
        s_own = jnp.where(kpos[None, :] <= qpos[:, None], s_own, NEG_INF)
        p = jax.nn.softmax(jnp.concatenate([s_own, s_sel], axis=-1), axis=-1).astype(vh.dtype)
        p_own = p[..., :MOBA_BLOCK]
        p_sel = p[..., MOBA_BLOCK:].reshape(B, H, MOBA_QCHUNK, topk, MOBA_BLOCK)
        return (jnp.einsum("bhqk,bhkd->bhqd", p_own, vown)
                + jnp.einsum("bhqnk,bhqnkd->bhqd", p_sel, vsel))

    out = lax.map(step, jnp.arange(sp // MOBA_QCHUNK))
    out = out.transpose(1, 0, 3, 2, 4).reshape(B, sp, H, dh)
    return out[:, :S]

def moba_mixer(xn, w_qkv, w_o, cos, sin):
    B, S, _ = xn.shape
    qkv = (xn @ w_qkv).reshape(B, S, 3, N_HEADS, HEAD_DIM)
    q = apply_rope(qkv[:, :, 0], cos, sin)
    k = apply_rope(qkv[:, :, 1], cos, sin)
    o = moba_attention(q, k, qkv[:, :, 2])
    return o.reshape(B, S, N_HEADS * HEAD_DIM) @ w_o

def causal_attention_blocked(q, k, v, scale):
    B, S, H, dk = q.shape
    dv = v.shape[-1]
    nq = S // ATTN_QBLOCK
    qb = q.reshape(B, nq, ATTN_QBLOCK, H, dk).transpose(1, 0, 2, 3, 4)
    key_pos = jnp.arange(S)

    def step(args):
        i, qi = args
        s = jnp.einsum("bqhd,bkhd->bhqk", qi, k, preferred_element_type=jnp.float32) * scale
        qpos = i * ATTN_QBLOCK + jnp.arange(ATTN_QBLOCK)
        s = jnp.where(key_pos[None, :] <= qpos[:, None], s, NEG_INF)
        p = jax.nn.softmax(s, axis=-1).astype(v.dtype)
        return jnp.einsum("bhqk,bkhd->bqhd", p, v)

    out = lax.map(step, (jnp.arange(nq), qb))
    return out.transpose(1, 0, 2, 3, 4).reshape(B, S, H, dv)

def mla_mixer(xn, w_in, q_norm, w_uq, kv_norm, w_ukv, w_o, cos_r, sin_r):
    B, S, _ = xn.shape
    c = xn @ w_in
    cq = rms_norm(c[..., :MLA_Q_LORA], q_norm)
    ckv = rms_norm(c[..., MLA_Q_LORA:MLA_Q_LORA + MLA_KV_LORA], kv_norm)
    kr = c[..., MLA_Q_LORA + MLA_KV_LORA:]
    qf = (cq @ w_uq).reshape(B, S, MLA_HEADS, MLA_NOPE + MLA_ROPE)
    q_rope = apply_rope(qf[..., MLA_NOPE:], cos_r, sin_r)
    kv = (ckv @ w_ukv).reshape(B, S, MLA_HEADS, MLA_NOPE + MLA_V)
    k_rope = jnp.broadcast_to(apply_rope(kr[:, :, None, :], cos_r, sin_r), (B, S, MLA_HEADS, MLA_ROPE))
    q = jnp.concatenate([qf[..., :MLA_NOPE], q_rope], axis=-1)
    k = jnp.concatenate([kv[..., :MLA_NOPE], k_rope], axis=-1)
    v = kv[..., MLA_NOPE:]
    o = causal_attention_blocked(q, k, v, (MLA_NOPE + MLA_ROPE) ** -0.5)
    return o.reshape(B, S, MLA_HEADS * MLA_V) @ w_o

def dilated_group_attention(q, k, v, window, dilation):
    B, S, H, dh = q.shape
    scale = dh ** -0.5
    span = window // dilation
    unit = DIL_BLOCK * dilation
    sp = -(-S // unit) * unit
    L = sp // dilation
    nb = L // DIL_BLOCK
    padw = ((0, 0), (0, sp - S), (0, 0), (0, 0))

    def to_blocks(t):
        t = jnp.pad(t, padw).reshape(B, L, dilation, H, dh).transpose(0, 3, 2, 1, 4)
        return t.reshape(B, H, dilation, nb, DIL_BLOCK, dh)

    def with_prev(t):
        prev = jnp.pad(t, ((0, 0), (0, 0), (0, 0), (1, 0), (0, 0), (0, 0)))[:, :, :, :-1]
        return jnp.concatenate([prev, t], axis=4)

    qb = to_blocks(q)
    kk = with_prev(to_blocks(k))
    vv = with_prev(to_blocks(v))
    s = jnp.einsum("bhrnqd,bhrnkd->bhrnqk", qb, kk, preferred_element_type=jnp.float32) * scale
    qi = jnp.arange(DIL_BLOCK)[:, None]
    kj = jnp.arange(2 * DIL_BLOCK)[None, :]
    dist = qi + DIL_BLOCK - kj
    key_sub = jnp.arange(nb)[:, None, None] * DIL_BLOCK - DIL_BLOCK + kj[None]
    mask = (dist >= 0)[None] & (dist <= span)[None] & (key_sub >= 0)
    s = jnp.where(mask, s, NEG_INF)
    lse = jax.nn.logsumexp(s, axis=-1)
    p = jnp.exp(s - lse[..., None]).astype(v.dtype)
    o = jnp.einsum("bhrnqk,bhrnkd->bhrnqd", p, vv)
    o = o.reshape(B, H, dilation, L, dh).transpose(0, 3, 2, 1, 4).reshape(B, sp, H, dh)[:, :S]
    lse = lse.reshape(B, H, dilation, L).transpose(0, 3, 2, 1).reshape(B, sp, H)[:, :S]
    return o, lse

def dilated_mixer(xn, w_qkv, w_o, cos, sin):
    B, S, _ = xn.shape
    G = len(DIL_GROUPS)
    qkv = (xn @ w_qkv).reshape(B, S, G, 3, DIL_HEADS, HEAD_DIM)
    outs, lses = [], []
    for g, (window, dilation) in enumerate(DIL_GROUPS):
        q = apply_rope(qkv[:, :, g, 0], cos, sin)
        k = apply_rope(qkv[:, :, g, 1], cos, sin)
        o, lse = dilated_group_attention(q, k, qkv[:, :, g, 2], window, dilation)
        outs.append(o)
        lses.append(lse)
    wts = jax.nn.softmax(jnp.stack(lses, axis=0), axis=0)
    o = jnp.einsum("gbsh,gbshd->bshd", wts, jnp.stack(outs, axis=0).astype(jnp.float32))
    return o.reshape(B, S, DIL_HEADS * HEAD_DIM).astype(xn.dtype) @ w_o

def stick_breaking_attention(q, k, v):
    B, S, H, dh = q.shape
    scale = dh ** -0.5
    nq = S // SB_QBLOCK
    qb = q.reshape(B, nq, SB_QBLOCK, H, dh).transpose(1, 0, 2, 3, 4)
    key_pos = jnp.arange(S)

    def step(args):
        i, qi = args
        z = jnp.einsum("bqhd,bkhd->bhqk", qi, k, preferred_element_type=jnp.float32) * scale
        qpos = i * SB_QBLOCK + jnp.arange(SB_QBLOCK)
        past = key_pos[None, :] < qpos[:, None]
        log_beta = jnp.where(past, jax.nn.log_sigmoid(z), NEG_INF)
        log_stay = jnp.where(past, jax.nn.log_sigmoid(-z), 0.0)
        after = jnp.concatenate([log_stay[..., 1:], jnp.zeros_like(log_stay[..., :1])], axis=-1)
        stay = lax.cumsum(after, axis=3, reverse=True)
        a = jnp.exp(log_beta + stay).astype(v.dtype)
        return jnp.einsum("bhqk,bkhd->bqhd", a, v)

    out = lax.map(step, (jnp.arange(nq), qb))
    return out.transpose(1, 0, 2, 3, 4).reshape(B, S, H, dh)

def stick_breaking_mixer(xn, w_qkv, w_o):
    B, S, _ = xn.shape
    qkv = (xn @ w_qkv).reshape(B, S, 3, SB_HEADS, HEAD_DIM)
    o = stick_breaking_attention(qkv[:, :, 0], qkv[:, :, 1], qkv[:, :, 2])
    return o.reshape(B, S, SB_HEADS * HEAD_DIM) @ w_o

def conv_ffn(xn, w_gate, conv_w, conv_b, w_up, w_down):
    S = xn.shape[1]
    g = xn @ w_gate
    gp = jnp.pad(g, ((0, 0), (CONV_WIDTH - 1, 0), (0, 0)))
    gc = conv_b + sum(conv_w[j] * gp[:, j:j + S] for j in range(CONV_WIDTH))
    h = jax.nn.gelu(gc, approximate=False) * (xn @ w_up)
    return h @ w_down

def _n_layers_of(kind):
    return len(range(kind, DEPTH, N_MIXERS))

def first_inputs(seed: int = 0) -> dict:
    key = jax.random.key(seed)
    ks = jax.random.split(key, 24)
    f32 = jnp.float32
    nA, nB, nC, nD = (_n_layers_of(m) for m in range(N_MIXERS))
    hd = N_HEADS * HEAD_DIM

    def dense(k, shape, fan_in):
        return jax.random.normal(k, shape, f32) * (fan_in ** -0.5)

    def gain(k, shape):
        return 1.0 + 0.02 * jax.random.normal(k, shape, f32)

    return {
        "x": jax.random.normal(ks[0], (BATCH, SEQ, D_MODEL), f32),
        "norm_mix": gain(ks[1], (DEPTH, D_MODEL)),
        "norm_ffn": gain(ks[2], (DEPTH, D_MODEL)),
        "norm_final": gain(ks[3], (D_MODEL,)),
        "a_w_qkv": dense(ks[4], (nA, D_MODEL, 3 * hd), D_MODEL),
        "a_w_o": dense(ks[5], (nA, hd, D_MODEL), hd),
        "b_w_in": dense(ks[6], (nB, D_MODEL, MLA_Q_LORA + MLA_KV_LORA + MLA_ROPE), D_MODEL),
        "b_q_norm": gain(ks[7], (nB, MLA_Q_LORA)),
        "b_w_uq": dense(ks[8], (nB, MLA_Q_LORA, MLA_HEADS * (MLA_NOPE + MLA_ROPE)), MLA_Q_LORA),
        "b_kv_norm": gain(ks[9], (nB, MLA_KV_LORA)),
        "b_w_ukv": dense(ks[10], (nB, MLA_KV_LORA, MLA_HEADS * (MLA_NOPE + MLA_V)), MLA_KV_LORA),
        "b_w_o": dense(ks[11], (nB, MLA_HEADS * MLA_V, D_MODEL), MLA_HEADS * MLA_V),
        "c_w_qkv": dense(ks[12], (nC, D_MODEL, len(DIL_GROUPS) * 3 * DIL_HEADS * HEAD_DIM), D_MODEL),
        "c_w_o": dense(ks[13], (nC, DIL_HEADS * HEAD_DIM, D_MODEL), DIL_HEADS * HEAD_DIM),
        "d_w_qkv": dense(ks[14], (nD, D_MODEL, 3 * SB_HEADS * HEAD_DIM), D_MODEL),
        "d_w_o": dense(ks[15], (nD, SB_HEADS * HEAD_DIM, D_MODEL), SB_HEADS * HEAD_DIM),
        "ffn_w_gate": dense(ks[16], (DEPTH, D_MODEL, D_FF), D_MODEL),
        "ffn_conv_w": dense(ks[17], (DEPTH, CONV_WIDTH, D_FF), CONV_WIDTH),
        "ffn_conv_b": 0.02 * jax.random.normal(ks[18], (DEPTH, D_FF), f32),
        "ffn_w_up": dense(ks[19], (DEPTH, D_MODEL, D_FF), D_MODEL),
        "ffn_w_down": dense(ks[20], (DEPTH, D_FF, D_MODEL), D_FF),
    }

def first_block(x, norm_mix, norm_ffn, norm_final,
              a_w_qkv, a_w_o,
              b_w_in, b_q_norm, b_w_uq, b_kv_norm, b_w_ukv, b_w_o,
              c_w_qkv, c_w_o,
              d_w_qkv, d_w_o,
              ffn_w_gate, ffn_conv_w, ffn_conv_b, ffn_w_up, ffn_w_down):
    S = x.shape[1]
    pos = jnp.arange(S, dtype=jnp.float32)
    cos_h, sin_h = rope_tables(pos, HEAD_DIM)
    cos_r, sin_r = rope_tables(pos, MLA_ROPE)
    h = x
    for i in range(DEPTH):
        kind, j = i % N_MIXERS, i // N_MIXERS
        hn = rms_norm(h, norm_mix[i])
        if kind == 0:
            mix = moba_mixer(hn, a_w_qkv[j], a_w_o[j], cos_h, sin_h)
        elif kind == 1:
            mix = mla_mixer(hn, b_w_in[j], b_q_norm[j], b_w_uq[j], b_kv_norm[j], b_w_ukv[j], b_w_o[j], cos_r, sin_r)
        elif kind == 2:
            mix = dilated_mixer(hn, c_w_qkv[j], c_w_o[j], cos_h, sin_h)
        else:
            mix = stick_breaking_mixer(hn, d_w_qkv[j], d_w_o[j])
        h = h + mix.astype(h.dtype)
        f = conv_ffn(rms_norm(h, norm_ffn[i]), ffn_w_gate[i], ffn_conv_w[i], ffn_conv_b[i], ffn_w_up[i], ffn_w_down[i])
        h = h + f.astype(h.dtype)
    return rms_norm(h, norm_final)


CHUNK = 64
N_MIXERS_2 = 2
POOL_WINDOWS = (2, 4, 8, 16)
POOL_GROUPS = len(POOL_WINDOWS)
POOL_GW = D_MODEL // POOL_GROUPS
N_HEADS_2 = 16
HEAD_DIM_2 = D_MODEL // N_HEADS_2
LEFT_CHUNKS = 8
BAND_CHUNKS = LEFT_CHUNKS + 1
BAND = BAND_CHUNKS * CHUNK
REL_CLIP = 256
D_FF_2 = 2816
CONV_W = 3
N_A = (DEPTH + 1) // 2
N_B = DEPTH // 2
EPS = 1e-6


def rmsnorm(x, g):
    xf = x.astype(jnp.float32)
    y = xf * lax.rsqrt(jnp.mean(xf * xf, axis=-1, keepdims=True) + EPS)
    return (y * g.astype(jnp.float32)).astype(x.dtype)

def pool_mixer(h, w_pool, b_pool, scale):
    B, S, D = h.shape
    hf = h.astype(jnp.float32)
    csp = jnp.concatenate([jnp.zeros((B, 1, D), jnp.float32), jnp.cumsum(hf, axis=1)], axis=1)
    t = jnp.arange(S)
    outs = []
    for g, w in enumerate(POOL_WINDOWS):
        c = csp[:, :, g * POOL_GW:(g + 1) * POOL_GW]
        upper = c[:, 1:]
        lower = jnp.concatenate([jnp.zeros((B, w - 1, POOL_GW), jnp.float32), c[:, :S - w + 1]], axis=1)
        cnt = jnp.minimum(t + 1, w).astype(jnp.float32)[None, :, None]
        outs.append((upper - lower) / cnt)
    pooled = jnp.concatenate(outs, axis=-1)
    y = (pooled - hf).astype(h.dtype).reshape(B, S, POOL_GROUPS, POOL_GW)
    y = jnp.einsum('bsgc,gcd->bsgd', y, w_pool).reshape(B, S, D) + b_pool
    return y * scale

def head_rmsnorm(x, g):
    xf = x.astype(jnp.float32)
    y = xf * lax.rsqrt(jnp.mean(xf * xf, axis=-1, keepdims=True) + EPS)
    return (y * g.astype(jnp.float32)).astype(x.dtype)

def chunk_attention(h, w_qkv, q_norm, k_norm, rel_table, w_o):
    B, S, D = h.shape
    nc = S // CHUNK
    qkv = h @ w_qkv
    q, k, v = jnp.split(qkv, 3, axis=-1)
    q = head_rmsnorm(q.reshape(B, S, N_HEADS_2, HEAD_DIM_2), q_norm)
    k = head_rmsnorm(k.reshape(B, S, N_HEADS_2, HEAD_DIM_2), k_norm)
    v = v.reshape(B, S, N_HEADS_2, HEAD_DIM_2)
    q = q.reshape(B, nc, CHUNK, N_HEADS_2, HEAD_DIM_2)
    pad = jnp.zeros((B, LEFT_CHUNKS, CHUNK, N_HEADS_2, HEAD_DIM_2), k.dtype)
    kp = jnp.concatenate([pad, k.reshape(B, nc, CHUNK, N_HEADS_2, HEAD_DIM_2)], axis=1)
    vp = jnp.concatenate([pad, v.reshape(B, nc, CHUNK, N_HEADS_2, HEAD_DIM_2)], axis=1)
    rel = jnp.arange(CHUNK)[:, None] - jnp.arange(BAND)[None, :] + LEFT_CHUNKS * CHUNK
    idx = jnp.clip(rel, -REL_CLIP, REL_CLIP) + REL_CLIP
    bias = rel_table.astype(jnp.float32)[:, idx]
    band_chunk = jnp.repeat(jnp.arange(BAND_CHUNKS), CHUNK)
    scale = HEAD_DIM_2 ** -0.5

    def one_chunk(c):
        qc = lax.dynamic_index_in_dim(q, c, axis=1, keepdims=False)
        kb = lax.dynamic_slice_in_dim(kp, c, BAND_CHUNKS, axis=1).reshape(B, BAND, N_HEADS_2, HEAD_DIM_2)
        vb = lax.dynamic_slice_in_dim(vp, c, BAND_CHUNKS, axis=1).reshape(B, BAND, N_HEADS_2, HEAD_DIM_2)
        s = jnp.einsum('bqhd,bkhd->bhqk', qc, kb).astype(jnp.float32) * scale + bias[None]
        valid = (band_chunk + c - LEFT_CHUNKS) >= 0
        s = jnp.where(valid[None, None, None, :], s, -1e30)
        p = jax.nn.softmax(s, axis=-1).astype(vb.dtype)
        return jnp.einsum('bhqk,bkhd->bqhd', p, vb)

    o = lax.map(one_chunk, jnp.arange(nc))
    o = jnp.transpose(o, (1, 0, 2, 3, 4)).reshape(B, S, D)
    return o @ w_o

def conv_ffn_2(h, w_gate, w_val, conv_w, conv_b, w_out):
    S = h.shape[1]
    a = h @ w_gate
    ap = jnp.pad(a, ((0, 0), (CONV_W - 1, 0), (0, 0)))
    a = ap[:, 0:S] * conv_w[0] + ap[:, 1:S + 1] * conv_w[1] + ap[:, 2:S + 2] * conv_w[2] + conv_b
    return (jax.nn.silu(a) * (h @ w_val)) @ w_out

def second_inputs(seed: int = 0) -> dict:
    key = jax.random.key(seed)
    ks = jax.random.split(key, 16)
    f32 = jnp.float32
    D, F = D_MODEL, D_FF_2
    nrm = lambda k, shape, s: jax.random.normal(k, shape, f32) * s
    return {
        "x": nrm(ks[0], (BATCH, SEQ, D), 1.0),
        "mix_norm": 1.0 + nrm(ks[1], (DEPTH, D), 0.02),
        "ffn_norm": 1.0 + nrm(ks[2], (DEPTH, D), 0.02),
        "pool_w": nrm(ks[3], (N_A, POOL_GROUPS, POOL_GW, POOL_GW), POOL_GW ** -0.5),
        "pool_b": nrm(ks[4], (N_A, D), 0.02),
        "pool_scale": 1.0 + nrm(ks[5], (N_A, D), 0.1),
        "attn_wqkv": nrm(ks[6], (N_B, D, 3 * D), D ** -0.5),
        "attn_q_norm": 1.0 + nrm(ks[7], (N_B, HEAD_DIM_2), 0.02),
        "attn_k_norm": 1.0 + nrm(ks[8], (N_B, HEAD_DIM_2), 0.02),
        "attn_rel_bias": nrm(ks[9], (N_B, N_HEADS_2, 2 * REL_CLIP + 1), 0.1),
        "attn_wo": nrm(ks[10], (N_B, D, D), D ** -0.5),
        "ffn_w_gate": nrm(ks[11], (DEPTH, D, F), D ** -0.5),
        "ffn_w_val": nrm(ks[12], (DEPTH, D, F), D ** -0.5),
        "ffn_conv_w": nrm(ks[13], (DEPTH, CONV_W, F), CONV_W ** -0.5),
        "ffn_conv_b": nrm(ks[14], (DEPTH, F), 0.02),
        "ffn_w_out": nrm(ks[15], (DEPTH, F, D), F ** -0.5),
    }

def second_block(x, mix_norm, ffn_norm, pool_w, pool_b, pool_scale, attn_wqkv, attn_q_norm,
              attn_k_norm, attn_rel_bias, attn_wo, ffn_w_gate, ffn_w_val, ffn_conv_w,
              ffn_conv_b, ffn_w_out):
    for i in range(DEPTH):
        h = rmsnorm(x, mix_norm[i])
        j = i // N_MIXERS_2
        if i % N_MIXERS_2 == 0:
            x = x + pool_mixer(h, pool_w[j], pool_b[j], pool_scale[j])
        else:
            x = x + chunk_attention(h, attn_wqkv[j], attn_q_norm[j], attn_k_norm[j],
                                    attn_rel_bias[j], attn_wo[j])
        h = rmsnorm(x, ffn_norm[i])
        x = x + conv_ffn_2(h, ffn_w_gate[i], ffn_w_val[i], ffn_conv_w[i], ffn_conv_b[i], ffn_w_out[i])
    return x


def setup_inputs(seed=0):
    out = dict(first_inputs(seed))
    for name, value in second_inputs(seed + 1).items():
        if name != "x":
            out[name + "_2"] = value
    return out


def reference(
    x, norm_mix, norm_ffn, norm_final, a_w_qkv, a_w_o, b_w_in, b_q_norm, b_w_uq, b_kv_norm,
    b_w_ukv, b_w_o, c_w_qkv, c_w_o, d_w_qkv, d_w_o, ffn_w_gate, ffn_conv_w, ffn_conv_b,
    ffn_w_up, ffn_w_down, mix_norm_2, ffn_norm_2, pool_w_2, pool_b_2, pool_scale_2, attn_wqkv_2,
    attn_q_norm_2, attn_k_norm_2, attn_rel_bias_2, attn_wo_2, ffn_w_gate_2, ffn_w_val_2,
    ffn_conv_w_2, ffn_conv_b_2, ffn_w_out_2,
):
    x = first_block(
        x, norm_mix, norm_ffn, norm_final, a_w_qkv, a_w_o, b_w_in, b_q_norm, b_w_uq, b_kv_norm,
        b_w_ukv, b_w_o, c_w_qkv, c_w_o, d_w_qkv, d_w_o, ffn_w_gate, ffn_conv_w, ffn_conv_b,
        ffn_w_up, ffn_w_down,
    )
    return second_block(
        x, mix_norm_2, ffn_norm_2, pool_w_2, pool_b_2, pool_scale_2, attn_wqkv_2, attn_q_norm_2,
        attn_k_norm_2, attn_rel_bias_2, attn_wo_2, ffn_w_gate_2, ffn_w_val_2, ffn_conv_w_2,
        ffn_conv_b_2, ffn_w_out_2,
    )


_drawn_inputs = setup_inputs


def setup_inputs(seed=0):
    import zlib

    import numpy as np

    out = dict(_drawn_inputs(seed))
    spreads = {}
    factors = {'norm_mix': 4.531,
     'b_q_norm': 8.0,
     'b_kv_norm': 8.0,
     'ffn_conv_b': 3.134,
     'mix_norm_2': 3.622,
     'ffn_norm_2': 3.356,
     'pool_b_2': 2.757,
     'attn_q_norm_2': 8.0,
     'attn_k_norm_2': 8.0,
     'attn_rel_bias_2': 5.712,
     'ffn_conv_b_2': 4.837}
    for name, (base, spread) in spreads.items():
        noise = np.random.default_rng([zlib.crc32(name.encode()), seed]).standard_normal(out[name].shape)
        drawn = base * np.exp(spread * noise) if base else spread * noise
        out[name] = jnp.asarray(drawn.astype(out[name].dtype))
    for name, factor in factors.items():
        out[name] = (out[name] * factor).astype(out[name].dtype)
    return out
```

```python
from contextlib import ExitStack

import numpy as np

import concourse.bass as bass
from concourse import mybir

F32 = mybir.dt.float32
F32R = mybir.dt.float32r
I32 = mybir.dt.int32
ALU = mybir.AluOpType
ACT = mybir.ActivationFunctionType
AX_X = mybir.AxisListType.X

S, D, KD = 256, 1024, 8
NF = 22
NG = 4
UNIT = 2048
RAW, RING = 2, 5
LOOK = 3
EPS = 1e-6
MAGIC = 1597463007.0

VECS = [("norm_mix", 16), ("norm_ffn", 16), ("norm_final", 8), ("mix_norm_2", 16), ("ffn_norm_2", 16),
        ("pool_b", 8), ("pool_scale", 8), ("b_q_norm", 3), ("b_kv_norm", 2), ("q_norm", 1), ("k_norm", 1),
        ("conv_w", 4 * 3 * NF), ("conv_b", 4 * NF)]
VEC_AT, VEC_N = {}, 0
for _name, _n in VECS:
    VEC_AT[_name] = VEC_N
    VEC_N += _n

CONSTS = [("ident", 128), ("cos0", 128), ("sin0", 128), ("cos1", 64), ("sin1", 64), ("mask0", 384),
          ("mask3", 384), ("icnt", 4 * S)]
CON_AT, CON_N = {}, 0
for _name, _n in CONSTS:
    CON_AT[_name] = CON_N
    CON_N += _n


def unit_plan():
    plan = []

    def qkv(name):
        for g in range(4):
            for part in range(3):
                plan.append((name, part * 4 + g, KD, 256))

    def out(name):
        for m in range(4):
            plan.append((name, m, KD, 256))

    def ffn(layer):
        for i in range(11):
            plan.append((f"gate{layer}", i, KD, 256))
            plan.append((f"up{layer}", i, KD, 256))
        for m in range(4):
            for c, nk in enumerate((8, 8, 6)):
                plan.append((f"down{layer}_{c}", m, nk, 256))

    qkv("a_qkv")
    out("a_o")
    ffn(0)
    plan.append(("b_in", 0, KD, 256))
    plan.append(("b_in", 1, KD, 256))
    plan.append(("b_in2", 0, KD, 160))
    for g in range(4):
        plan.append(("b_uq", g, 3, 384))
        plan.append(("b_ukv", g, 2, 512))
    out("b_o")
    ffn(1)
    plan.append(("pool", 0, KD, 256))
    ffn(2)
    qkv("d_qkv")
    out("d_o")
    ffn(3)
    return plan


class Engine:

    def __init__(self, name, sem):
        self.name, self.sem, self.n, self.queue, self.seen = name, sem, 0, [], {}

    def wait(self, *tokens):
        for t in tokens:
            if t is None:
                continue
            sem, value = t
            if self.seen.get(id(sem), 0) < value:
                self.seen[id(sem)] = value
                self.queue.append(lambda e, sem=sem, value=value: e.wait_ge(sem, value))

    def do(self, fn, *tokens):
        self.wait(*tokens)
        self.n += 1
        self.queue.append(lambda e: fn(e).then_inc(self.sem, 1))
        return (self.sem, self.n)

    def quiet(self, fn, *tokens):
        self.wait(*tokens)
        self.queue.append(fn)

    def now(self):
        return (self.sem, self.n)

    def play(self, e):
        for fn in self.queue:
            fn(e)


def build(nc, dram, out):
    plan = unit_plan()
    with ExitStack() as ctx:
        def sb(name, shape, dt=F32, stack=ctx):
            return stack.enter_context(nc.sbuf_tensor(name, shape, dt))

        def sem(name):
            return ctx.enter_context(nc.semaphore(name))

        PE = Engine("pe", sem("s_pe"))
        AC = Engine("act", sem("s_act"))
        DV = Engine("dve", sem("s_dve"))
        PO = Engine("pool", sem("s_pool"))
        SP = Engine("sp", sem("s_sp"))
        s_raw = [sem(f"s_raw{i}") for i in range(RAW)]
        s_con, s_x, s_vec, s_out = sem("s_con"), sem("s_x"), sem("s_vec"), sem("s_out")
        s_bias = [sem("s_bias0"), sem("s_bias1")]

        raw = [sb(f"raw{i}", [128, UNIT]) for i in range(RAW)]
        whi = [sb(f"whi{i}", [128, UNIT], F32R) for i in range(RING)]
        wlo = [sb(f"wlo{i}", [128, UNIT], F32R) for i in range(RING)]
        xT = sb("xT", [128, KD, S])
        xh = sb("xh", [128, KD, S], F32R)
        xl = sb("xl", [128, KD, S], F32R)
        con = sb("con", [128, CON_N])
        vec = sb("vec", [128, VEC_N])
        ones = sb("ones", [128, 128])
        sq = sb("sq", [128, 2, S])
        ssum = sb("ssum", [128, 2, S])
        rb = sb("rb", [128, S])
        small = sb("small", [128, 16, 16])

        dg = sb("dg", [128, 2, 128])
        crs = sb("crs", [128, 2, 2, 64])
        rtmp = sb("rtmp", [128, 2, 256])

        ffn_mem = ExitStack()
        hh = sb("hh", [128, NF, S], F32R, ffn_mem)
        hl = sb("hl", [128, NF, S], F32R, ffn_mem)
        gp = [sb(f"gp{i}", [128, 2, S + 2], F32, ffn_mem) for i in range(2)]
        ct = sb("ct", [128, 2, S], F32, ffn_mem)
        ub = sb("ub", [128, 2, S], F32, ffn_mem)
        hb = sb("hb", [128, 2, S], F32, ffn_mem)
        ffn_mem.close()

        att_mem = ExitStack()
        oh = sb("oh", [128, KD, S], F32R, att_mem)
        ol = sb("ol", [128, KD, S], F32R, att_mem)
        vv = sb("vv", [128, 2, D], F32, att_mem)
        n1 = sb("n1", [128, 2, 384], F32, att_mem)
        n2 = sb("n2", [128, 2, 384], F32, att_mem)
        sc = sb("sc", [128, 2, 384], F32, att_mem)
        pt = sb("pt", [128, 2, 384], F32, att_mem)
        two = ExitStack()
        qT = [sb(f"qT{i}", [128, 2, S], F32, two) for i in range(2)]
        kT = [sb(f"kT{i}", [128, 2, S], F32, two) for i in range(2)]
        bm = [sb(f"bm{i}", [128, 4, 384], F32, two) for i in range(2)]
        bw = [sb(f"bw{i}", [128, 4, S], F32, two) for i in range(1)]
        two.close()
        mla = ExitStack()
        qM = [sb(f"qM{i}", [96, 4, S], F32, mla) for i in range(1)]
        kM = [sb(f"kM{i}", [96, 4, S], F32, mla) for i in range(1)]
        cc = sb("cc", [128, 2, 672], F32, mla)
        kr = sb("kr", [128, 2, 32], F32, mla)
        ch = sb("ch", [128, 5, S], F32R, mla)
        cl = sb("cl", [128, 5, S], F32R, mla)
        mla.close()
        att_mem.close()

        pool_mem = ExitStack()
        ph = sb("ph", [128, KD, S + 16], F32, pool_mem)
        pa = [sb(f"pa{i}", [128, 2, S + 16], F32, pool_mem) for i in range(4)]
        pool_mem.close()

        bank = [ctx.enter_context(nc.psum_tensor(f"bank{i}", [128, 512], F32)) for i in range(4)]
        SB = ctx.enter_context(nc.psum_tensor("SB", [128, 2, 512], F32))
        TB = ctx.enter_context(nc.psum_tensor("TB", [128, 2, 512], F32))

        def cst(name):
            n = dict(CONSTS)[name]
            return con[:, CON_AT[name]:CON_AT[name] + n]

        def vcol(name, i):
            return vec[:, VEC_AT[name] + i:VEC_AT[name] + i + 1]

        ident = cst("ident")

        t_x, t_vec, t_con = (s_x, 16), (s_vec, 16), (s_con, 16)
        SP.quiet(lambda e: e.dma_start(xT[:, :, :], dram["x"]).then_inc(s_x, 16))
        SP.quiet(lambda e: e.dma_start(vec[:, :], dram["vec"]).then_inc(s_vec, 16))
        t_ones = DV.do(lambda e: e.memset(ones[:, :], 1.0))

        hi_t, lo_t, used = {}, {}, {}
        stream = {"dma": 0, "hi": 0, "lo": 0}

        def load_unit():
            n = stream["dma"]
            if n >= len(plan):
                return
            name, i, nk, w = plan[n]
            SP.wait(lo_t.get(n - RAW))
            SP.quiet(lambda e: e.dma_start(raw[n % RAW][:, 0:nk * w], dram[name][i]).then_inc(s_raw[n % RAW], 16))
            stream["dma"] += 1

        def raw_here(n):
            return (s_raw[n % RAW], 16 * (n // RAW + 1))

        def split_hi():
            n = stream["hi"]
            if n >= len(plan):
                return
            _, _, nk, w = plan[n]
            hi_t[n] = AC.do(lambda e: e.activation(whi[n % RING][:, 0:nk * w], raw[n % RAW][:, 0:nk * w], ACT.Copy),
                            raw_here(n), used.get(n - RING))
            stream["hi"] += 1

        def split_lo():
            n = stream["lo"]
            if n >= stream["hi"]:
                return
            _, _, nk, w = plan[n]
            lo_t[n] = DV.do(lambda e: e.tensor_tensor(wlo[n % RING][:, 0:nk * w], raw[n % RAW][:, 0:nk * w],
                                                      whi[n % RING][:, 0:nk * w].bitcast(F32), ALU.subtract),
                            hi_t[n], raw_here(n), used.get(n - RING))
            stream["lo"] += 1
            load_unit()

        def ahead(n):
            while stream["hi"] < min(len(plan), n + LOOK + 1):
                split_hi()
                split_lo()

        def unit(n):
            _, _, nk, w = plan[n]
            r = n % RING
            return (whi[r][:, 0:nk * w].rearrange("p (k n) -> p k n", k=nk),
                    wlo[r][:, 0:nk * w].rearrange("p (k n) -> p k n", k=nk))

        at = {"unit": 0}

        def next_unit():
            at["unit"] += 1
            return at["unit"] - 1

        free = [[] for _ in range(4)]
        turn = {"n": 0}
        held = set()

        def take():
            while True:
                b = turn["n"] % 4
                turn["n"] += 1
                if b not in held:
                    return b

        def hold():
            b = take()
            held.add(b)
            return b

        def three(po, ah, al, bh, bl, start, stop, tokens=(), done=False):
            PE.quiet(lambda e: e.matmul(po, ah, bh, start=start, stop=False, skip_group_check=True), *tokens)
            PE.quiet(lambda e: e.matmul(po, ah, bl, start=False, stop=False, skip_group_check=True))
            last = lambda e: e.matmul(po, al, bh, start=False, stop=stop, skip_group_check=True)
            if done:
                return PE.do(last)
            PE.quiet(last)

        def tensorT(n, b, k0, k1, ch_t, act_h, act_l, first, last, kk=0, mt=2):
            wh, wl = unit(n)
            po = bank[b][:, :].rearrange("p (m s) -> p m s", m=2)
            tok = None
            for k in range(k0, k1):
                for m in range(mt):
                    end = last and k == k1 - 1
                    waits = [hi_t[n], lo_t[n], *ch_t(k + kk)] + (free[b] if first and k == k0 and m == 0 else [])
                    tok = three(po[:, m, :], wh[:, k, m * 128:(m + 1) * 128], wl[:, k, m * 128:(m + 1) * 128],
                                act_h[:, k + kk, :], act_l[:, k + kk, :],
                                start=(first and k == k0 and m == 0), stop=end,
                                tokens=waits, done=(k == k1 - 1 and m == mt - 1))
            return tok

        x_t = [None] * KD
        xs_t = [[None, None] for _ in range(KD)]

        def split_x(k, gain, gi):
            g = vcol(gain, gi)
            a = AC.do(lambda e: e.activation(xh[:, k, :], xT[:, k, :], ACT.Copy, scale=g), x_t[k], t_vec, PE.now())
            d = DV.do(lambda e: e.scalar_tensor_tensor(out=xl[:, k, :], in0=xT[:, k, :], scalar=g,
                                                       in1=xh[:, k, :].bitcast(F32), op0=ALU.mult,
                                                       op1=ALU.subtract), a)
            xs_t[k] = [a, d]

        ss_t = {"t": None}
        sq_free = {"t": None}

        def squares(c):
            if c == 0:
                ss_t["t"] = AC.do(lambda e: e.activation(ssum[:, :, :], xT[:, 0:2, :], ACT.Square),
                                  x_t[0], x_t[1], PE.now())
                return
            a = AC.do(lambda e: e.activation(sq[:, :, :], xT[:, 2 * c:2 * c + 2, :], ACT.Square),
                      x_t[2 * c], x_t[2 * c + 1], sq_free["t"])
            ss_t["t"] = sq_free["t"] = DV.do(
                lambda e: e.tensor_tensor(ssum[:, :, :], ssum[:, :, :], sq[:, :, :], ALU.add), a, ss_t["t"])

        def rsqrt(v, y, t, tok):
            tok = DV.do(lambda e: e.tensor_scalar(t.bitcast(I32), v.bitcast(I32), 1, None,
                                                  ALU.logical_shift_right), tok)
            tok = DV.do(lambda e: e.tensor_scalar(y.bitcast(I32), t.bitcast(I32), -1.0, MAGIC, ALU.mult,
                                                  ALU.add), tok)
            for _ in range(3):
                tok = DV.do(lambda e: e.scalar_tensor_tensor(out=t, in0=y, scalar=-0.5, in1=v, op0=ALU.mult,
                                                             op1=ALU.mult), tok)
                tok = DV.do(lambda e: e.tensor_tensor(t, t, y, ALU.mult), tok)
                tok = DV.do(lambda e: e.scalar_tensor_tensor(out=y, in0=t, scalar=1.5, in1=y, op0=ALU.add,
                                                             op1=ALU.mult), tok)
            return tok

        rcol, rv, rt = small[:, 0, 0:2], small[:, 1, 0:2], small[:, 2, 0:2]
        r_t = {"col": None, "row": None}

        def rms_col():
            b = take()
            for h in range(2):
                for c in range(2):
                    fn = lambda e, h=h, c=c: e.matmul(bank[b][:, h:h + 1], ssum[:, c, h * 128:(h + 1) * 128],
                                                      ones[:, 0:1], start=(h == 0 and c == 0), stop=(c == 1),
                                                      skip_group_check=True)
                    if h == 1 and c == 1:
                        m = PE.do(fn)
                    else:
                        PE.quiet(fn, ss_t["t"], t_ones, *free[b])
            v = DV.do(lambda e: e.tensor_scalar(rv, bank[b][:, 0:2], 1.0 / D, EPS, ALU.mult, ALU.add), m, AC.now(),
                      PE.now())
            free[b] = [v]
            r_t["col"] = rsqrt(rv, rcol, rt, v)

        def rms_row():
            for h in range(2):
                t = DV.do(lambda e, h=h: e.tensor_scalar(dg[:, h, :], ident, rcol[:, h:h + 1], None, ALU.mult),
                          r_t["col"], t_con, PE.now())
            b = take()
            PE.quiet(lambda e: e.matmul(bank[b][:, 0:128], ones[:, :], dg[:, 0, :], start=True, stop=True,
                                        skip_group_check=True), t, *free[b])
            m = PE.do(lambda e: e.matmul(bank[b][:, 128:256], ones[:, :], dg[:, 1, :], start=True, stop=True,
                                         skip_group_check=True))
            r_t["row"] = DV.do(lambda e: e.tensor_copy(rb[:, :], bank[b][:, 0:256]), m)
            free[b] = [r_t["row"]]

        def residual(b, c, tok, gain=None, gi=0, sums=True):
            r = DV.do(lambda e: e.tensor_tensor(xT[:, 2 * c:2 * c + 2, :].rearrange("p k s -> p (k s)"),
                                                bank[b][:, :], xT[:, 2 * c:2 * c + 2, :].rearrange("p k s -> p (k s)"),
                                                ALU.add), tok, *xs_t[2 * c], *xs_t[2 * c + 1], AC.now())
            free[b] = [r]
            x_t[2 * c] = x_t[2 * c + 1] = r
            if sums:
                squares(c)
            if gain:
                for k in (2 * c, 2 * c + 1):
                    split_x(k, gain, gi + k)

        def ffn(layer, func, next_gain, next_gi):
            cw = lambda tap, f: vcol("conv_w", (layer * 3 + tap) * NF + f)
            cb = lambda f: vcol("conv_b", layer * NF + f)
            h_t = [None] * NF
            late = []
            xw = lambda k: xs_t[k]
            for i in range(2):
                pads = DV.do(lambda e, i=i: e.memset(gp[i][:, :, 0:2], 0.0), PE.now(), AC.now())

            def act_part(i, bg, bu, tg, tu):
                g = gp[i % 2]
                rbb = rb[:, :].unsqueeze(1).to_broadcast([128, 2, S])
                pg = bank[bg][:, :].rearrange("p (m s) -> p m s", m=2)
                pu = bank[bu][:, :].rearrange("p (m s) -> p m s", m=2)
                d0 = DV.do(lambda e: e.tensor_tensor(g[:, :, 2:S + 2], pg, rbb, ALU.mult), tg, r_t["row"], pads)
                free[bg] = [d0]
                while late:
                    late.pop(0)()
                a0 = AC.do(lambda e: e.activation(ct[:, 0, :], g[:, 0, 0:S], ACT.Identity, scale=cw(0, 2 * i),
                                                  bias=cb(2 * i)), d0, h_t[2 * i - 2] if i else None)
                a1 = AC.do(lambda e: e.activation(ct[:, 1, :], g[:, 1, 0:S], ACT.Identity, scale=cw(0, 2 * i + 1),
                                                  bias=cb(2 * i + 1)), d0)
                split_lo()
                d1 = DV.do(lambda e: e.tensor_tensor(ub[:, :, :], pu, rbb, ALU.mult), tu)
                free[bu] = [d1]
                for tap in (1, 2):
                    for m, a in ((0, a0), (1, a1)):
                        d = DV.do(lambda e, tap=tap, m=m: e.scalar_tensor_tensor(
                            out=ct[:, m, :], in0=g[:, m, tap:S + tap], scalar=cw(tap, 2 * i + m), in1=ct[:, m, :],
                            op0=ALU.mult, op1=ALU.add), a, DV_last[m])
                        DV_last[m] = d
                a2 = AC.do(lambda e: e.activation(ct[:, :, :], ct[:, :, :], func), *DV_last)
                split_hi()

                def finish():
                    d3 = DV.do(lambda e: e.tensor_tensor(hb[:, :, :], ct[:, :, :], ub[:, :, :], ALU.mult), a2, d1)
                    a3 = AC.do(lambda e: e.activation(hh[:, 2 * i:2 * i + 2, :], hb[:, :, :], ACT.Copy), d3)
                    d4 = DV.do(lambda e: e.tensor_tensor(hl[:, 2 * i:2 * i + 2, :], hb[:, :, :],
                                                         hh[:, 2 * i:2 * i + 2, :].bitcast(F32), ALU.subtract), a3)
                    h_t[2 * i] = h_t[2 * i + 1] = d3
                    hs_t[2 * i] = hs_t[2 * i + 1] = [a3, d4]
                late.append(finish)
                split_lo()

            DV_last = [None, None]
            hs_t = [[None, None]] * NF
            hs_t = list(hs_t)
            for i in range(11):
                n0, n1_ = next_unit(), next_unit()
                ahead(n0)
                ahead(n1_) if i == 0 else None
                bg, bu = take(), take()
                if i == 0:
                    for k in range(KD):
                        tg = tensorT(n0, bg, k, k + 1, xw, xh, xl, k == 0, k == KD - 1)
                        tu = tensorT(n1_, bu, k, k + 1, xw, xh, xl, k == 0, k == KD - 1)
                        if k == 5:
                            rms_col()
                    used[n0] = used[n1_] = tu
                    rms_row()
                else:
                    tg = used[n0] = tensorT(n0, bg, 0, KD, xw, xh, xl, True, True)
                    ahead(n1_)
                    tu = used[n1_] = tensorT(n1_, bu, 0, KD, xw, xh, xl, True, True)
                act_part(i, bg, bu, tg, tu)
            while late:
                late.pop(0)()
            for c in range(4):
                b = take()
                k0 = 0
                for j, nk in enumerate((8, 8, 6)):
                    n = next_unit()
                    ahead(n)
                    t = used[n] = tensorT(n, b, 0, nk, lambda k: hs_t[k], hh, hl, j == 0, j == 2, kk=k0)
                    k0 += nk
                residual(b, c, t, next_gain, next_gi)

        def natural(n, banks, act_h, act_l, act_t, halves=None):
            wh, wl = unit(n)
            _, _, nk, w = plan[n]
            toks = []
            for h in (range(2) if halves is None else halves):
                b = banks[h % len(banks)]
                po = bank[b][:, 0:w] if len(banks) == 2 else bank[b][:, h * 256:h * 256 + w]
                new = len(banks) == 2 or h == 0
                for k in range(nk):
                    waits = [hi_t[n], lo_t[n], *act_t(k)] + (free[b] if k == 0 and new else [])
                    sl = slice(h * 128, (h + 1) * 128)
                    tok = three(po, act_h[:, k, sl], act_l[:, k, sl], wh[:, k, :], wl[:, k, :],
                                start=(k == 0), stop=(k == nk - 1), tokens=waits, done=(k == nk - 1))
                toks.append(tok)
            return toks

        mxs, nms, lsum, linv = (small[:, i, 0:4] for i in (3, 4, 5, 6))
        sc_free = {"t": []}
        pt_t, o_t = {}, {}
        s_free, tb_free, pt_free = {"t": []}, {"t": []}, {"t": []}
        p_t = {}
        v_t = {}

        def scores(j, heads, scale, mask, m_t):
            for a, (q, k, toks) in enumerate(heads):
                PE.quiet(lambda e, a=a, q=q, k=k: e.matmul(SB[:, a, 0:128], q[:, 0:128], k[:, 0:128], start=True,
                                                           stop=True, skip_group_check=True), *toks, *s_free["t"])
                m = PE.do(lambda e, a=a, q=q, k=k: e.matmul(SB[:, a, 128:384], q[:, 128:256], k[:, 0:256],
                                                            start=True, stop=True, skip_group_check=True))
            d = DV.do(lambda e: e.scalar_tensor_tensor(out=sc[:, :, :], in0=SB[:, :, 0:384], scalar=scale, in1=mask,
                                                       op0=ALU.mult, op1=ALU.add), m, *m_t, *sc_free["t"])
            s_free["t"] = [d]
            d1 = DV.do(lambda e: e.tensor_reduce(mxs[:, 0:2], sc[:, :, 0:128], AX_X, ALU.max), d)
            d2 = DV.do(lambda e: e.tensor_reduce(mxs[:, 2:4], sc[:, :, 128:384], AX_X, ALU.max), d)
            d3 = DV.do(lambda e: e.tensor_scalar(nms, mxs, -1.0, None, ALU.mult), d1, d2)
            for a in range(2):
                for h, sl in ((0, slice(0, 128)), (1, slice(128, 384))):
                    x = AC.do(lambda e, a=a, h=h, sl=sl: e.activation(
                        sc[:, a, sl], sc[:, a, sl], ACT.Exp, bias=nms[:, 2 * h + a:2 * h + a + 1],
                        accum_out=lsum[:, 2 * h + a:2 * h + a + 1]), d3)
            p_t[j] = x

        def normalize(j):
            d = DV.do(lambda e: e.reciprocal(linv, lsum), p_t[j])
            for a in range(2):
                for h, sl in ((0, slice(0, 128)), (1, slice(128, 384))):
                    x = DV.do(lambda e, a=a, h=h, sl=sl: e.tensor_scalar(
                        sc[:, a, sl], sc[:, a, sl], linv[:, 2 * h + a:2 * h + a + 1], None, ALU.mult), d)
            p_t[j] = x

        def transposes(j):
            for a in range(2):
                for c in range(3):
                    m = PE.do(lambda e, a=a, c=c: e.transpose(TB[:, a, c * 128:(c + 1) * 128],
                                                              sc[:, a, c * 128:(c + 1) * 128], ident),
                              p_t[j], *tb_free["t"])
            sc_free["t"] = [m]
            x = AC.do(lambda e: e.activation(pt[:, :, :], TB[:, :, 0:384], ACT.Copy), m, *pt_free["t"])
            tb_free["t"] = [x]
            pt_t[j] = x

        def values(j):
            b = take()
            for a in range(2):
                o = slice(64 * a, 64 * a + 64)
                col = slice((2 * j + a) * 64, (2 * j + a) * 64 + 64)
                PE.quiet(lambda e, a=a, o=o, col=col: e.matmul(bank[b][o, 0:128], vv[:, 0, col], pt[:, a, 0:128],
                                                               start=True, stop=True, skip_group_check=True),
                         pt_t[j], *v_t[j // 2], *free[b])
                PE.quiet(lambda e, a=a, o=o, col=col: e.matmul(bank[b][o, 128:256], vv[:, 0, col], pt[:, a, 128:256],
                                                               start=True, stop=False, skip_group_check=True))
                m = PE.do(lambda e, a=a, o=o, col=col: e.matmul(bank[b][o, 128:256], vv[:, 1, col],
                                                                pt[:, a, 256:384], start=False, stop=True,
                                                                skip_group_check=True))
            pt_free["t"] = [m]
            a_ = AC.do(lambda e: e.activation(oh[:, j, :], bank[b][:, 0:256], ACT.Copy), m)
            d_ = DV.do(lambda e: e.tensor_tensor(ol[:, j, :], bank[b][:, 0:256], oh[:, j, :].bitcast(F32),
                                                 ALU.subtract), a_)
            free[b] = [a_, d_]
            o_t[j] = [a_, d_]

        def project_out(gain, gi, sums=True):
            n0, n1_ = next_unit(), next_unit()
            bb = [None, None]
            st = {}
            ow = lambda k: o_t[k]

            def piece(ks):
                def run():
                    for k in ks:
                        if k == 0:
                            ahead(n0)
                            ahead(n1_)
                            st["b"] = (hold(), hold())
                        b0, b1 = st["b"]
                        st["t0"] = tensorT(n0, b0, k, k + 1, ow, oh, ol, k == 0, k == KD - 1)
                        st["t1"] = tensorT(n1_, b1, k, k + 1, ow, oh, ol, k == 0, k == KD - 1)
                return run

            def finish():
                used[n0] = used[n1_] = st["t1"]
                held.clear()
                residual(st["b"][0], 0, st["t1"], gain, gi, sums)
                residual(st["b"][1], 1, st["t1"], gain, gi, sums)
                for c in (2, 3):
                    n = next_unit()
                    ahead(n)
                    b = take()
                    t = used[n] = tensorT(n, b, 0, KD, ow, oh, ol, True, True)
                    residual(b, c, t, gain, gi, sums)
            return [piece([0, 1]), piece([2, 3]), piece([4]), piece([5]), piece([6])], piece([7]), finish

        def heads_mixer(kind, gain, gi):
            last = {}
            rc = {}

            def begin():
                rms_col()
                if kind == 0:
                    for h in range(2):
                        for nm, c in (("cos0", 0), ("sin0", 1)):
                            rc["t"] = DV.do(lambda e, h=h, nm=nm, c=c: e.tensor_scalar(
                                crs[:, c, h, :], cst(nm)[:, h * 64:(h + 1) * 64], rcol[:, h:h + 1], None, ALU.mult),
                                r_t["col"], t_con)

            def group(g):
                ns = [next_unit() for _ in range(3)]
                st = {}

                def half(part, h):
                    def run():
                        n = ns[part]
                        if h == 0:
                            ahead(n)
                            st[part] = hold()
                        st[part, h] = natural(n, [st[part]], xh, xl, lambda k: xs_t[k], halves=[h])[0]
                        if h == 1:
                            used[n] = st[part, 1]
                            held.discard(st[part])
                            if g == 0 and part == 0:
                                begin()
                            evacuate(part)
                    return run

                def evacuate(part):
                    b, t = st[part], st[part, 1]
                    if part == 2:
                        for h in range(2):
                            a = AC.do(lambda e, h=h: e.activation(vv[:, h, g * 256:(g + 1) * 256],
                                                                  bank[b][:, h * 256:(h + 1) * 256], ACT.Copy,
                                                                  scale=rcol[:, h:h + 1]), t, r_t["col"])
                        free[b] = [a]
                        v_t[g] = [a]
                        return
                    dst = n1 if part == 0 else n2
                    flat = dst[:, :, 0:256]
                    if kind == 0:
                        tmp = rtmp
                        ps = bank[b][:, :].rearrange("p (t h d) -> p t h d", t=2, h=4)
                        fl = flat.rearrange("p t (h d) -> p t h d", h=4)
                        tm = tmp[:, :, 0:256].rearrange("p t (h d) -> p t h d", h=4)
                        wide = lambda c, lo, n: crs[:, c, :, lo:lo + n].unsqueeze(2).to_broadcast([128, 2, 4, n])
                        for q in range(2):
                            src = slice(32 - 32 * q, 64 - 32 * q)
                            d1 = DV.do(lambda e, q=q, src=src: e.tensor_tensor(
                                tm[:, :, :, 32 * q:32 * q + 32], ps[:, :, :, src], wide(1, 32 * q, 32), ALU.mult),
                                t, rc["t"], last.get("tmp"))
                        for h in range(2):
                            d0 = DV.do(lambda e, h=h: e.tensor_tensor(
                                fl[:, h], ps[:, h], crs[:, 0, h, :].unsqueeze(1).to_broadcast([128, 4, 64]),
                                ALU.mult), t, rc["t"], last.get(part))
                        free[b] = [d0, d1]
                        d = DV.do(lambda e: e.tensor_tensor(flat, flat, tmp[:, :, 0:256], ALU.add), d0, d1)
                        last["tmp"] = d
                        st["n", part] = d
                    else:
                        for h in range(2):
                            a = AC.do(lambda e, h=h: e.activation(flat[:, h, :], bank[b][:, h * 256:(h + 1) * 256],
                                                                  ACT.Copy, scale=rcol[:, h:h + 1]),
                                      t, r_t["col"], last.get(part))
                        free[b] = [a]
                        x = AC.do(lambda e: e.activation(rtmp[:, :, 0:256], flat, ACT.Square), a, last.get("tmp"))
                        ss = small[:, 7, 0:8]
                        vs = small[:, 8, 0:8]
                        ys = small[:, 9 + part, 0:8]
                        tt = small[:, 11, 0:8]
                        d = DV.do(lambda e: e.tensor_reduce(
                            ss.rearrange("p (t h) -> p t h", t=2),
                            rtmp[:, :, 0:256].rearrange("p t (h d) -> p t h d", h=4), AX_X, ALU.add), x)
                        last["tmp"] = d
                        d = DV.do(lambda e: e.tensor_scalar(vs, ss, 1.0 / 64, EPS, ALU.mult, ALU.add), d)
                        d = rsqrt(vs, ys, tt, d)
                        for h in range(2):
                            f4 = flat[:, h, :].rearrange("p (h d) -> p h d", h=4)
                            st["n", part] = DV.do(lambda e, h=h, f4=f4: e.tensor_tensor(
                                f4, f4, ys[:, 4 * h:4 * h + 4].unsqueeze(2).to_broadcast([128, 4, 64]), ALU.mult), d)

                def turn_over(part):
                    def run():
                        src = n1 if part == 0 else n2
                        dst = (qT if part == 0 else kT)[g % 2]
                        b = take()
                        for c in range(2):
                            for h in range(2):
                                m = PE.do(lambda e, c=c, h=h: e.transpose(
                                    bank[b][:, c * 256 + h * 128:c * 256 + (h + 1) * 128],
                                    src[:, h, c * 128:(c + 1) * 128], ident), st["n", part], t_con, *free[b])
                        last[part] = m
                        kw = {"scale": vcol("q_norm" if part == 0 else "k_norm", 0)} if kind == 3 else {}
                        a = AC.do(lambda e: e.activation(dst[:, :, :].rearrange("p c s -> p (c s)"), bank[b][:, :],
                                                         ACT.Copy, **kw), m, PE.now())
                        free[b] = [a]
                        tt_t[g, part] = a
                    return run

                def bias():
                    if kind == 3:
                        load = (s_bias[0], 16 * (g + 1))
                        SP.wait(bw_free["t"], bm_t.get(g - 1))
                        SP.quiet(lambda e: e.dma_start(bw[0][:, :, :], dram["bias"][g]).then_inc(s_bias[0], 16))
                        m3 = cst("mask3")
                        p0 = PO.do(lambda e: e.tensor_tensor(
                            bm[g % 2][:, :, 0:128], bw[0][:, :, 128:256],
                            m3[:, 0:128].unsqueeze(1).to_broadcast([128, 4, 128]), ALU.add),
                            load, t_con, sc_read[g - 2] if g >= 2 else None)
                        p1 = PO.do(lambda e: e.tensor_tensor(
                            bm[g % 2][:, :, 128:384], bw[0][:, :, :],
                            m3[:, 128:384].unsqueeze(1).to_broadcast([128, 4, 256]), ALU.add))
                        bm_t[g] = p1
                bias()
                return [half(0, 0), half(0, 1), half(1, 0), turn_over(0), half(1, 1), half(2, 0), turn_over(1),
                        half(2, 1)]

            tt_t, bm_t, sc_read = {}, {}, {}
            bw_free = {"t": PE.now()}

            def pair_heads(j):
                g, c = j // 2, j % 2
                tk = [tt_t[g, 0], tt_t[g, 1]]
                return [(qT[g % 2][64 * a:64 * a + 64, c, :], kT[g % 2][64 * a:64 * a + 64, c, :], tk)
                        for a in range(2)]

            def mask_of(j):
                if kind == 0:
                    return cst("mask0").unsqueeze(1).to_broadcast([128, 2, 384]), [t_con]
                g, c = j // 2, j % 2
                return bm[g % 2][:, 2 * c:2 * c + 2, :], [bm_t[g]]

            for p in group(0):
                p()
            sc_free["t"] = [PE.now()]
            for g in range(4):
                if g < 3:
                    f = group(g + 1)
                else:
                    f, seven, fin = project_out(gain, gi)
                for j in (2 * g, 2 * g + 1):
                    attention_step(j, pair_heads, 0.125, mask_of, f, g)
                sc_read[g] = DV.now()
            values(7)
            seven()
            fin()

        def attention_step(j, pair_heads, scale, mask_of, f, g):
            def fill(n):
                for _ in range(n):
                    if f:
                        f.pop(0)()
            mask, m_t = mask_of(j)
            scores(j, pair_heads(j), scale, mask, m_t)
            if j:
                values(j - 1)
            if g < 3:
                fill(2)
                normalize(j)
                fill(2 if j % 2 == 0 else 1)
                transposes(j)
                fill(0 if j % 2 == 0 else 1)
            else:
                fill(1)
                normalize(j)
                fill(1)
                transposes(j)
                fill(0 if j % 2 == 0 else 1)


        def latent_mixer(gain, gi):
            tcol = small[:, 12, 0:4]
            c_t = {}
            banks_of = {}
            ns = [next_unit() for _ in range(3)]
            ahead(ns[0])
            for i, n in enumerate(ns):
                ahead(n)
                w = plan[n][3]
                b = take()
                t = used[n] = natural(n, [b], xh, xl, lambda k: xs_t[k])[-1]
                if i == 0:
                    rms_col()
                for h in range(2):
                    a = AC.do(lambda e, h=h, b=b, i=i, w=w: e.activation(
                        cc[:, h, i * 256:i * 256 + w], bank[b][:, h * 256:h * 256 + w], ACT.Copy,
                        scale=rcol[:, h:h + 1]), t, r_t["col"])
                free[b] = [a]
                c_t[i] = a
                if i:
                    latent_chunks(c_t[i - 1], (0, 1) if i == 1 else (2, 3))
            latent_chunks(c_t[2], (4,))
            lv, ly, lt = small[:, 13, 0:4], small[:, 14, 0:4], small[:, 15, 0:4]
            for h in range(2):
                AC.do(lambda e, h=h: e.activation(n1[:, 0, 0:384], cc[:, h, 0:384], ACT.Square,
                                                  accum_out=tcol[:, h:h + 1]), c_t[2], AC.now())
                a = AC.do(lambda e, h=h: e.activation(n1[:, 1, 0:256], cc[:, h, 384:640], ACT.Square,
                                                      accum_out=tcol[:, 2 + h:3 + h]), AC.now())
            d = DV.do(lambda e: e.tensor_scalar(lv[:, 0:2], tcol[:, 0:2], 1.0 / 384, EPS, ALU.mult, ALU.add), a)
            d = DV.do(lambda e: e.tensor_scalar(lv[:, 2:4], tcol[:, 2:4], 1.0 / 256, EPS, ALU.mult, ALU.add), a)
            l_t = rsqrt(lv, ly, lt, d)
            cs, sn = (cst(x).rearrange("p (t d) -> p t d", t=2) for x in ("cos1", "sin1"))
            krs = cc[:, :, 640:672]
            d = DV.do(lambda e: e.tensor_tensor(kr[:, :, :], krs, cs, ALU.mult), c_t[2], t_con)
            tmp = rtmp[:, :, 0:32]
            d1 = DV.do(lambda e: e.tensor_tensor(tmp[:, :, 0:16], krs[:, :, 16:32], sn[:, :, 0:16], ALU.mult))
            d1 = DV.do(lambda e: e.tensor_tensor(tmp[:, :, 16:32], krs[:, :, 0:16], sn[:, :, 16:32], ALU.mult))
            kr_t = DV.do(lambda e: e.tensor_tensor(kr[:, :, :], kr[:, :, :], tmp, ALU.add), d, d1)
            kr_p = PO
            last = {}
            tt_t = {}

            def group(g):
                nq, nkv = next_unit(), next_unit()
                st = {}
                cur = lambda x: x[0]

                def q_half(h):
                    def run():
                        if h == 0:
                            ahead(nq)
                        b = take()
                        t = natural(nq, [b, b], ch, cl, lambda k: cs_t[k], halves=[h])[0]
                        if h == 1:
                            used[nq] = t
                        a = AC.do(lambda e: e.activation(n1[:, h, :], bank[b][:, 0:384], ACT.Copy,
                                                         scale=ly[:, h:h + 1]), t, l_t, last.get("q"))
                        free[b] = [a]
                        if h == 1:
                            nr = n1[:, :, :].rearrange("p t (h d) -> p t h d", h=4)[:, :, :, 64:96]
                            tm = rtmp[:, :, 0:128].rearrange("p t (h d) -> p t h d", h=4)
                            wide = lambda x, lo, n: x[:, :, lo:lo + n].unsqueeze(2).to_broadcast([128, 2, 4, n])
                            d1 = DV.do(lambda e: e.tensor_tensor(tm[:, :, :, 0:16], nr[:, :, :, 16:32],
                                                                 wide(sn, 0, 16), ALU.mult), a, DV.now())
                            d1 = DV.do(lambda e: e.tensor_tensor(tm[:, :, :, 16:32], nr[:, :, :, 0:16],
                                                                 wide(sn, 16, 16), ALU.mult))
                            for tt in range(2):
                                d0 = DV.do(lambda e, tt=tt: e.tensor_tensor(
                                    nr[:, tt], nr[:, tt], cs[:, tt, :].unsqueeze(1).to_broadcast([128, 4, 32]),
                                    ALU.mult), d1)
                            for tt in range(2):
                                d = DV.do(lambda e, tt=tt: e.tensor_tensor(nr[:, tt], nr[:, tt], tm[:, tt],
                                                                           ALU.add), d0, d1)
                            st["q"] = d
                    return run

                def kv_half(h):
                    def run():
                        if h == 0:
                            ahead(nkv)
                        b = take()
                        t = natural(nkv, [b, b], ch[:, 3:5, :], cl[:, 3:5, :], lambda k: cs_t[3 + k], halves=[h])[0]
                        if h == 1:
                            used[nkv] = t
                        pv = bank[b][:, :].rearrange("p (h d) -> p h d", h=4)
                        k4 = n2[:, h, :].rearrange("p (h d) -> p h d", h=4)
                        a = AC.do(lambda e: e.activation(k4[:, :, 0:64], pv[:, :, 0:64], ACT.Copy,
                                                         scale=ly[:, 2 + h:3 + h]), t, l_t, last.get("k"))
                        a = AC.do(lambda e: e.activation(
                            vv[:, h, g * 256:(g + 1) * 256].rearrange("p (h d) -> p h d", h=4), pv[:, :, 64:128],
                            ACT.Copy, scale=ly[:, 2 + h:3 + h]))
                        free[b] = [a]
                        p = PO.do(lambda e: e.tensor_copy(k4[:, :, 64:96],
                                                          kr[:, h, :].unsqueeze(1).to_broadcast([128, 4, 32])),
                                  kr_t, last.get("k"))
                        st["k", h] = [a, p]
                        v_t[g] = [a]
                    return run

                def turn_over(part, c):
                    def run():
                        src = n1 if part == 0 else n2
                        dst = (qM if part == 0 else kM)[0]
                        b = take()
                        toks = [st["q"]] if part == 0 else st["k", 0] + st["k", 1]
                        for a_ in range(2):
                            for h in range(2):
                                hd = 2 * c + a_
                                m = PE.do(lambda e, a_=a_, h=h, hd=hd: e.transpose(
                                    bank[b][0:96, a_ * 256 + h * 128:a_ * 256 + (h + 1) * 128],
                                    src[:, h, hd * 96:(hd + 1) * 96], ident), *toks, t_con, *free[b])
                        last["q" if part == 0 else "k"] = m
                        a = AC.do(lambda e: e.activation(dst[:, 2 * c:2 * c + 2, :].rearrange("p c s -> p (c s)"),
                                                         bank[b][0:96, :], ACT.Copy), m, PE.now())
                        free[b] = [a]
                        tt_t[g, part, c] = a
                    return run
                return ([q_half(0), q_half(1), kv_half(0), kv_half(1)],
                        [turn_over(0, 0), turn_over(1, 0), turn_over(0, 1), turn_over(1, 1)])

            def pair_heads(j):
                g, c = j // 2, j % 2
                tk = [tt_t[g, 0, c], tt_t[g, 1, c]]
                return [(qM[0][:, 2 * c + a, :], kM[0][:, 2 * c + a, :], tk) for a in range(2)]

            mask_of = lambda j: (cst("mask0").unsqueeze(1).to_broadcast([128, 2, 384]), [t_con])
            for p in sum(group(0), []):
                p()
            for g in range(4):
                if g < 3:
                    proj, turns = group(g + 1)
                else:
                    proj, seven, fin = project_out(gain, gi)
                    turns = []
                for j in (2 * g, 2 * g + 1):
                    mask, m_t = mask_of(j)
                    scores(j, pair_heads(j), 96 ** -0.5, mask, m_t)
                    if j:
                        values(j - 1)
                    for _ in range(2 if g < 3 or j % 2 == 0 else 2):
                        if proj:
                            proj.pop(0)()
                    normalize(j)
                    if g == 3 and proj:
                        proj.pop(0)()
                    transposes(j)
                for p in turns:
                    p()
            values(7)
            for p in proj:
                p()
            seven()
            fin()

        cs_t = {}

        def latent_chunks(tok, chunks):
            for c in chunks:
                b = take()
                for h in range(2):
                    m = PE.do(lambda e, h=h, c=c, b=b: e.transpose(bank[b][:, h * 128:(h + 1) * 128],
                                                                   cc[:, h, c * 128:(c + 1) * 128], ident),
                              tok, t_con, *free[b])
                g = vcol("b_q_norm", c) if c < 3 else vcol("b_kv_norm", c - 3)
                a = AC.do(lambda e, c=c, b=b, g=g: e.activation(ch[:, c, :], bank[b][:, 0:256], ACT.Copy, scale=g), m)
                d = DV.do(lambda e, c=c, b=b, g=g: e.scalar_tensor_tensor(
                    out=cl[:, c, :], in0=bank[b][:, 0:256], scalar=g, in1=ch[:, c, :].bitcast(F32), op0=ALU.mult,
                    op1=ALU.subtract), a)
                free[b] = [a, d]
                cs_t[c] = [a, d]

        def pool_mixer(gi, next_gain, next_gi):
            n = next_unit()
            ahead(n)
            ahead(n + 1)
            rms_col()
            rms_row()
            z = PO.do(lambda e: e.memset(ph[:, :, 0:16], 0.0), PE.now(), AC.now(), DV.now())
            for i in range(4):
                z = PO.do(lambda e, i=i: e.memset(pa[i][:, :, 0:16], 0.0))
            bs = small[:, 3, 0:8]
            t_bs = DV.do(lambda e: e.tensor_tensor(bs, vec[:, VEC_AT["pool_b"]:VEC_AT["pool_b"] + 8],
                                                   vec[:, VEC_AT["pool_scale"]:VEC_AT["pool_scale"] + 8], ALU.mult),
                         t_vec, PE.now(), AC.now())
            order = (1, 3, 0, 2)
            h_t = {}
            for g in order:
                for k in (2 * g, 2 * g + 1):
                    h_t[g] = DV.do(lambda e, k=k: e.scalar_tensor_tensor(
                        out=ph[:, k, 16:S + 16], in0=xT[:, k, :], scalar=vcol("mix_norm_2", gi + k), in1=rb[:, :],
                        op0=ALU.mult, op1=ALU.mult), x_t[k], r_t["row"], PE.now())
            icnt = cst("icnt").rearrange("p (g s) -> p g s", g=4)
            y_t = {}
            for g in order:
                E = PO if g < 2 else DV
                src = ph[:, 2 * g:2 * g + 2, :]
                bufs = pa[0:2] if g < 2 else pa[2:4]
                tok = h_t[g]
                for lvl in range(g + 1):
                    sh = 1 << lvl
                    dst = bufs[lvl % 2]
                    tok = E.do(lambda e, src=src, dst=dst, sh=sh: e.tensor_tensor(
                        dst[:, :, 16:S + 16], src[:, :, 16:S + 16], src[:, :, 16 - sh:S + 16 - sh], ALU.add),
                        tok, z, E.now())
                    src = dst
                out_ = bufs[(g + 1) % 2]
                tok = E.do(lambda e, src=src, out_=out_, g=g: e.tensor_tensor(
                    out_[:, :, 16:S + 16], src[:, :, 16:S + 16], icnt[:, g, :].unsqueeze(1).to_broadcast([128, 2, S]),
                    ALU.mult), tok, t_con)
                dst_ = ph[:, 2 * g:2 * g + 2, :]
                y_t[g] = E.do(lambda e, out_=out_, dst_=dst_: e.tensor_tensor(
                    dst_[:, :, 16:S + 16], out_[:, :, 16:S + 16], dst_[:, :, 16:S + 16], ALU.subtract), tok)
            wh, wl = unit(n)
            for g in order:
                a = AC.do(lambda e, g=g: e.activation(xh[:, 2 * g:2 * g + 2, :], ph[:, 2 * g:2 * g + 2, 16:S + 16],
                                                      ACT.Copy), y_t[g], PE.now())
                d = DV.do(lambda e, g=g: e.tensor_tensor(xl[:, 2 * g:2 * g + 2, :], ph[:, 2 * g:2 * g + 2, 16:S + 16],
                                                         xh[:, 2 * g:2 * g + 2, :].bitcast(F32), ALU.subtract), a)
                for k in (2 * g, 2 * g + 1):
                    xs_t[k] = [a, d]
            done_t = []
            for g in order:
                b = take()
                for k in (0, 1):
                    for m in range(2):
                        t = three(bank[b][:, m * 256:(m + 1) * 256], wh[:, 2 * g + k, m * 128:(m + 1) * 128],
                                  wl[:, 2 * g + k, m * 128:(m + 1) * 128], xh[:, 2 * g + k, :], xl[:, 2 * g + k, :],
                                  start=(k == 0 and m == 0), stop=(k == 1),
                                  tokens=[hi_t[n], lo_t[n], *xs_t[2 * g + k], *free[b]], done=(k == 1 and m == 1))
                done_t.append((g, b, t))
            used[n] = t
            for g, b, t in done_t:
                for m in range(2):
                    k = 2 * g + m
                    d = DV.do(lambda e, k=k: e.tensor_scalar(xT[:, k, :], xT[:, k, :], bs[:, k:k + 1], None, ALU.add),
                              t_bs, h_t[g], AC.now())
                    d = DV.do(lambda e, k=k, m=m, b=b: e.scalar_tensor_tensor(
                        out=xT[:, k, :], in0=bank[b][:, m * 256:(m + 1) * 256], scalar=vcol("pool_scale", k),
                        in1=xT[:, k, :], op0=ALU.mult, op1=ALU.add), t, d)
                    x_t[k] = d
                free[b] = [d]
            for c in range(4):
                squares(c)
                for k in (2 * c, 2 * c + 1):
                    split_x(k, next_gain, next_gi + k)

        DV.queue_start = None
        for _ in range(RAW):
            load_unit()
        SP.quiet(lambda e: e.dma_start(con[:, :], dram["con"]).then_inc(s_con, 16))
        for k in range(KD):
            x_t[k] = t_x
        for c in range(4):
            for k in (2 * c, 2 * c + 1):
                split_x(k, "norm_mix", k)
            squares(c)
        heads_mixer(0, "norm_ffn", 0)
        ffn(0, ACT.Gelu, "norm_mix", 8)
        latent_mixer("norm_ffn", 8)
        ffn(1, ACT.Gelu, None, 0)
        rms_col()
        rms_row()
        for k in range(KD):
            x_t[k] = DV.do(lambda e, k=k: e.scalar_tensor_tensor(
                out=xT[:, k, :], in0=xT[:, k, :], scalar=vcol("norm_final", k), in1=rb[:, :], op0=ALU.mult,
                op1=ALU.mult), r_t["row"], x_t[k], AC.now())
        for c in range(4):
            squares(c)
        pool_mixer(0, "ffn_norm_2", 0)
        ffn(2, ACT.Silu, "mix_norm_2", 8)
        heads_mixer(3, "ffn_norm_2", 8)
        ffn(3, ACT.Silu, None, 0)
        SP.wait(*x_t)
        SP.quiet(lambda e: e.dma_start(out, xT[:, :, :]).then_inc(s_out, 16))
        SP.quiet(lambda e: e.wait_ge(s_out, 16))

        block = ctx.enter_context(nc.Block())

        @block.sync
        def _(e):
            SP.play(e)

        @block.scalar
        def _(e):
            AC.play(e)

        @block.vector
        def _(e):
            DV.play(e)

        @block.gpsimd
        def _(e):
            PO.play(e)

        @block.tensor
        def _(e):
            PE.play(e)


def lay_units(w, cols, nk=None):
    k, n = w.shape
    v = w.reshape(k // 128, 128, n // cols, cols)
    return np.ascontiguousarray(v.transpose(2, 1, 0, 3)).reshape(n // cols, 128, k // 128 * cols)


def chan(v):
    return np.ascontiguousarray(v.reshape(-1, 128).T)


def constants():
    def rope(dim):
        inv = np.float32(10000.0) ** (-np.arange(0, dim, 2, dtype=np.float32) / np.float32(dim))
        ang = np.arange(S, dtype=np.float32)[:, None] * inv[None, :].astype(np.float32)
        c, s = np.cos(ang).astype(np.float32), np.sin(ang).astype(np.float32)
        lay = lambda a: a.reshape(2, 128, dim).transpose(1, 0, 2).reshape(128, 2 * dim)
        return lay(np.concatenate([c, c], 1)), lay(np.concatenate([-s, s], 1))

    p = np.arange(128)[:, None]
    c0, s0 = rope(64)
    c1, s1 = rope(32)
    k0, k1 = np.arange(128)[None, :], np.arange(256)[None, :]
    big = np.float32(-1e30)
    mask0 = np.concatenate([np.where(k0 <= p, 0, big), np.where(k1 <= p + 128, 0, big)], 1)
    mask3 = np.concatenate([np.where(k0 // 64 <= p // 64, 0, big),
                            np.where(k1 // 64 <= (p + 128) // 64, 0, big)], 1)
    t = np.arange(S)
    icnt = np.concatenate([1.0 / np.minimum(t + 1, w) for w in (2, 4, 8, 16)])[None, :].repeat(128, 0)
    return np.ascontiguousarray(np.concatenate([np.eye(128), c0, s0, c1, s1, mask0, mask3, icnt], 1),
                                dtype=np.float32)


def kernel(**inputs):
    import concourse.bacc as _bacc
    from concourse.bass_utils import run_bass_kernel_spmd as _run

    i = {k: np.asarray(v) for k, v in inputs.items()}
    a = {}
    a["x"] = i["x"][0].T.reshape(KD, 128, S).transpose(1, 0, 2)
    a["con"] = constants()
    a["vec"] = np.concatenate([
        chan(i["norm_mix"]), chan(i["norm_ffn"]), chan(i["norm_final"]), chan(i["mix_norm_2"]),
        chan(i["ffn_norm_2"]), chan(i["pool_b_2"]), chan(i["pool_scale_2"]), chan(i["b_q_norm"]),
        chan(i["b_kv_norm"]), chan(np.concatenate([i["attn_q_norm_2"], i["attn_q_norm_2"]], 1)),
        chan(np.concatenate([i["attn_k_norm_2"], i["attn_k_norm_2"]], 1)),
        chan(i["ffn_conv_w"]), chan(i["ffn_conv_w_2"]), chan(i["ffn_conv_b"]), chan(i["ffn_conv_b_2"])], 1)
    a["a_qkv"] = lay_units(i["a_w_qkv"][0], 256)
    a["a_o"] = lay_units(i["a_w_o"][0], 256)
    a["b_in"] = lay_units(i["b_w_in"][0][:, 0:512], 256)
    a["b_in2"] = lay_units(i["b_w_in"][0][:, 512:672], 160)
    a["b_uq"] = lay_units(i["b_w_uq"][0], 384)
    a["b_ukv"] = lay_units(i["b_w_ukv"][0], 512)
    a["b_o"] = lay_units(i["b_w_o"][0], 256)
    a["pool"] = i["pool_w_2"][0].reshape(8, 128, 256).transpose(1, 0, 2).reshape(1, 128, 2048)
    a["d_qkv"] = lay_units(i["attn_wqkv_2"][0], 256)
    a["d_o"] = lay_units(i["attn_wo_2"][0], 256)
    for layer in range(4):
        j = layer % 2
        g, u, d = (("ffn_w_gate", "ffn_w_up", "ffn_w_down"), ("ffn_w_gate_2", "ffn_w_val_2", "ffn_w_out_2"))[
            layer // 2]
        a[f"gate{layer}"] = lay_units(i[g][j], 256)
        a[f"up{layer}"] = lay_units(i[u][j], 256)
        for c, (k0, k1) in enumerate(((0, 1024), (1024, 2048), (2048, 2816))):
            a[f"down{layer}_{c}"] = lay_units(i[d][j][k0:k1], 256)
    idx = 384 + np.arange(128)[:, None] - np.arange(256)[None, :]
    a["bias"] = i["attn_rel_bias_2"][0][:, idx].reshape(4, 4, 128, 256).transpose(0, 2, 1, 3)
    a = {k: np.ascontiguousarray(v, dtype=v.dtype) for k, v in a.items()}

    nc = _bacc.Bacc("TRN2", target_bir_lowering=False, num_devices=1)
    dram = {k: nc.dram_tensor(f"in_{k}", v.shape, mybir.dt.from_np(v.dtype), kind="ExternalInput").ap()
            for k, v in a.items()}
    out = nc.dram_tensor("out_0", (128, KD, S), F32, kind="ExternalOutput").ap()
    build(nc, dram, out)
    r = _run(nc, [{f"in_{k}": v for k, v in a.items()}], core_ids=[0])
    got = r.results[0]["out_0"]
    return np.ascontiguousarray(got.transpose(1, 0, 2).reshape(D, S).T).reshape(1, S, D)
```

```python
from contextlib import ExitStack

import numpy as np

import concourse.bass as bass
from concourse import mybir

F32 = mybir.dt.float32
F32R = mybir.dt.float32r
I32 = mybir.dt.int32
ALU = mybir.AluOpType
ACT = mybir.ActivationFunctionType
AX_X = mybir.AxisListType.X

S, D, KD = 256, 1024, 8
NF = 22
NG = 4
UNIT = 2048
RAW, RING = 3, 5
LOOK = 2
EPS = 1e-6
MAGIC = 1597463007.0

VECS = [("norm_mix", 16), ("norm_ffn", 16), ("norm_final", 8), ("mix_norm_2", 16), ("ffn_norm_2", 16),
        ("pool_b", 8), ("pool_scale", 8), ("b_q_norm", 3), ("b_kv_norm", 2), ("q_norm", 1), ("k_norm", 1),
        ("conv_w", 4 * 3 * NF), ("conv_b", 4 * NF)]
VEC_AT, VEC_N = {}, 0
for _name, _n in VECS:
    VEC_AT[_name] = VEC_N
    VEC_N += _n

CONSTS = [("ident", 128), ("cos0", 128), ("sin0", 128), ("cos1", 64), ("sin1", 64), ("mask0", 384),
          ("mask3", 384), ("icnt", 64)]
CON_AT, CON_N = {}, 0
for _name, _n in CONSTS:
    CON_AT[_name] = CON_N
    CON_N += _n


def unit_plan():
    plan = []

    def qkv(name):
        unit = lambda part, g: plan.append((name, part * 4 + g, KD, 256))
        unit(1, 0)
        unit(0, 0)
        for g in range(4):
            if g < 3:
                unit(1, g + 1)
                unit(0, g + 1)
            unit(2, g)

    def out(name):
        for m in range(4):
            plan.append((name, m, KD, 256))

    def ffn(layer):
        for i in range(11):
            plan.append((f"gate{layer}", i, KD, 256))
            plan.append((f"up{layer}", i, KD, 256))
        for m in range(4):
            for c, nk in enumerate((8, 8, 6)):
                plan.append((f"down{layer}_{c}", m, nk, 256))

    qkv("a_qkv")
    out("a_o")
    ffn(0)
    plan.append(("b_in", 0, KD, 256))
    plan.append(("b_in", 1, KD, 256))
    plan.append(("b_in2", 0, KD, 160))
    for g in range(4):
        plan.append(("b_uq", g, 3, 384))
        plan.append(("b_ukv", g, 2, 512))
    out("b_o")
    ffn(1)
    plan.append(("pool", 0, KD, 256))
    ffn(2)
    qkv("d_qkv")
    out("d_o")
    ffn(3)
    return plan


class Engine:

    def __init__(self, name, sem):
        self.name, self.sem, self.n, self.queue, self.seen = name, sem, 0, [], {}

    def wait(self, *tokens):
        for t in tokens:
            if t is None:
                continue
            sem, value = t
            if self.seen.get(id(sem), 0) < value:
                self.seen[id(sem)] = value
                self.queue.append(lambda e, sem=sem, value=value: e.wait_ge(sem, value))

    def do(self, fn, *tokens):
        self.wait(*tokens)
        self.n += 1
        self.queue.append(lambda e: fn(e).then_inc(self.sem, 1))
        return (self.sem, self.n)

    def quiet(self, fn, *tokens):
        self.wait(*tokens)
        self.queue.append(fn)

    def now(self):
        return (self.sem, self.n)

    def play(self, e):
        for fn in self.queue:
            fn(e)


def build(nc, dram, out):
    plan = unit_plan()
    with ExitStack() as ctx:
        def sb(name, shape, dt=F32, stack=ctx):
            return stack.enter_context(nc.sbuf_tensor(name, shape, dt))

        def sem(name):
            return ctx.enter_context(nc.semaphore(name))

        PE = Engine("pe", sem("s_pe"))
        AC = Engine("act", sem("s_act"))
        DV = Engine("dve", sem("s_dve"))
        PO = Engine("pool", sem("s_pool"))
        SP = Engine("sp", sem("s_sp"))
        s_raw = [sem(f"s_raw{i}") for i in range(RAW)]
        s_con, s_x, s_vec, s_out, s_x2 = (sem(f"s_{x}") for x in ("con", "x", "vec", "out", "x2"))
        s_bias = [sem("s_bias0"), sem("s_bias1")]

        raw = [sb(f"raw{i}", [128, UNIT]) for i in range(RAW)]
        whi = [sb(f"whi{i}", [128, UNIT], F32R) for i in range(RING)]
        wlo = [sb(f"wlo{i}", [128, UNIT], F32R) for i in range(RING)]
        xT = sb("xT", [128, KD, S])
        xh = sb("xh", [128, KD, S], F32R)
        xl = sb("xl", [128, KD, S], F32R)
        con = sb("con", [128, CON_N])
        vec = sb("vec", [128, VEC_N])
        ones = sb("ones", [128, 128])
        sq = sb("sq", [128, 2, S])
        ssum = sb("ssum", [128, 2, S])
        rb = sb("rb", [128, S])
        small = sb("small", [128, 16, 16])

        dg = sb("dg", [128, 2, 128])
        crs = sb("crs", [128, 2, 2, 64])
        rtmp = sb("rtmp", [128, 2, 256])

        ffn_mem = ExitStack()
        hh = sb("hh", [128, NF, S], F32R, ffn_mem)
        hl = sb("hl", [128, NF, S], F32R, ffn_mem)
        gp = [sb(f"gp{i}", [128, 2, S + 2], F32, ffn_mem) for i in range(2)]
        ssum2 = sb("ssum2", [128, 2, S], F32, ffn_mem)
        sq2 = sb("sq2", [128, 2, S], F32, ffn_mem)
        cts = [sb(f"ct{i}", [128, 2, S], F32, ffn_mem) for i in range(2)]
        ubs = [sb(f"ub{i}", [128, 2, S], F32, ffn_mem) for i in range(2)]
        hb = sb("hb", [128, 2, S], F32, ffn_mem)
        ffn_mem.close()

        att_mem = ExitStack()
        oh = sb("oh", [128, KD, S], F32R, att_mem)
        ol = sb("ol", [128, KD, S], F32R, att_mem)
        vv = sb("vv", [128, 2, D], F32, att_mem)
        n1 = sb("n1", [128, 2, 384], F32, att_mem)
        n2 = sb("n2", [128, 2, 384], F32, att_mem)
        scs = [sb(f"sc{i}", [128, 2, 384], F32, att_mem) for i in range(3)]
        pt = sb("pt", [128, 2, 384], F32, att_mem)
        two = ExitStack()
        qT = [sb(f"qT{i}", [128, 2, S], F32, two) for i in range(2)]
        kT = [sb(f"kT{i}", [128, 2, S], F32, two) for i in range(2)]
        bm = [sb(f"bm{i}", [128, 4, 384], F32, two) for i in range(2)]
        bw = [sb(f"bw{i}", [128, 4, S], F32, two) for i in range(1)]
        two.close()
        mla = ExitStack()
        qM = [sb(f"qM{i}", [96, 4, S], F32, mla) for i in range(2)]
        kM = [sb(f"kM{i}", [96, 4, S], F32, mla) for i in range(2)]
        cc = sb("cc", [128, 2, 672], F32, mla)
        kr = sb("kr", [128, 2, 32], F32, mla)
        ch, cl = oh[:, 3:8, :], ol[:, 3:8, :]
        mla.close()
        att_mem.close()

        pool_mem = ExitStack()
        ph = sb("ph", [128, KD, S + 16], F32, pool_mem)
        rb2 = sb("rb2", [128, S], F32, pool_mem)
        fix = [sb(f"fix{i}", [128, 2, 16], F32, pool_mem) for i in range(4)]
        pa = [sb(f"pa{i}", [128, 2, S + 16], F32, pool_mem) for i in range(5)]
        pool_mem.close()

        bank = [ctx.enter_context(nc.psum_tensor(f"bank{i}", [128, 512], F32)) for i in range(4)]
        SB = ctx.enter_context(nc.psum_tensor("SB", [128, 2, 512], F32))
        TB = ctx.enter_context(nc.psum_tensor("TB", [128, 2, 512], F32))

        def cst(name):
            n = dict(CONSTS)[name]
            return con[:, CON_AT[name]:CON_AT[name] + n]

        def vcol(name, i):
            return vec[:, VEC_AT[name] + i:VEC_AT[name] + i + 1]

        ident = cst("ident")

        t_x, t_x2, t_vec, t_con = (s_x, 16), (s_x2, 16), (s_vec, 16), (s_con, 16)
        SP.quiet(lambda e: e.dma_start(vec[:, :], dram["vec"]).then_inc(s_vec, 16))
        SP.quiet(lambda e: e.dma_start(xT[:, 0:4, :], dram["x"][:, 0:4, :]).then_inc(s_x, 16))
        t_ones = DV.do(lambda e: e.memset(ones[:, :], 1.0))

        hi_t, lo_t, used = {}, {}, {}
        stream = {"dma": 0, "hi": 0, "lo": 0}

        def load_unit():
            n = stream["dma"]
            if n >= len(plan):
                return
            name, i, nk, w = plan[n]
            SP.wait(lo_t.get(n - RAW))
            SP.quiet(lambda e: e.dma_start(raw[n % RAW][:, 0:nk * w], dram[name][i]).then_inc(s_raw[n % RAW], 16))
            stream["dma"] += 1

        def raw_here(n):
            return (s_raw[n % RAW], 16 * (n // RAW + 1))

        def split_hi():
            n = stream["hi"]
            if n >= len(plan) or (n >= RING and n - RING not in used):
                return False
            _, _, nk, w = plan[n]
            hi_t[n] = AC.do(lambda e: e.activation(whi[n % RING][:, 0:nk * w], raw[n % RAW][:, 0:nk * w], ACT.Copy),
                            raw_here(n), used.get(n - RING))
            stream["hi"] += 1
            return True

        def split_lo():
            n = stream["lo"]
            if n >= stream["hi"]:
                return
            _, _, nk, w = plan[n]
            lo_t[n] = DV.do(lambda e: e.tensor_tensor(wlo[n % RING][:, 0:nk * w], raw[n % RAW][:, 0:nk * w],
                                                      whi[n % RING][:, 0:nk * w].bitcast(F32), ALU.subtract),
                            hi_t[n], raw_here(n), used.get(n - RING))
            stream["lo"] += 1
            load_unit()

        def ahead(n):
            if lazy["on"]:
                ready(n)
                lazy["n"] = n
                return
            while stream["hi"] < n + LOOK + 2 and split_hi():
                if stream["hi"] > 1:
                    split_lo()
            while stream["lo"] < min(stream["hi"], n + LOOK + 1):
                split_lo()

        lazy = {"on": False, "n": 0}

        def catch_up():
            if stream["hi"] < lazy["n"] + LOOK + 2:
                split_hi()
            if stream["lo"] < min(stream["hi"], lazy["n"] + LOOK + 1):
                split_lo()

        def ready(n):
            while stream["lo"] <= n:
                if stream["hi"] <= stream["lo"]:
                    assert split_hi()
                split_lo()

        def unit(n):
            _, _, nk, w = plan[n]
            r = n % RING
            return (whi[r][:, 0:nk * w].rearrange("p (k n) -> p k n", k=nk),
                    wlo[r][:, 0:nk * w].rearrange("p (k n) -> p k n", k=nk))

        at = {"unit": 0}

        def next_unit():
            at["unit"] += 1
            return at["unit"] - 1

        free = [[] for _ in range(4)]
        turn = {"n": 0}
        held = set()

        def take():
            while True:
                b = turn["n"] % 4
                turn["n"] += 1
                if b not in held:
                    return b

        def hold():
            b = take()
            held.add(b)
            return b

        def three(po, ah, al, bh, bl, start, stop, tokens=(), done=False):
            PE.quiet(lambda e: e.matmul(po, ah, bh, start=start, stop=False, skip_group_check=True), *tokens)
            PE.quiet(lambda e: e.matmul(po, ah, bl, start=False, stop=False, skip_group_check=True))
            last = lambda e: e.matmul(po, al, bh, start=False, stop=stop, skip_group_check=True)
            if done:
                return PE.do(last)
            PE.quiet(last)

        def tensorT(n, b, k0, k1, ch_t, act_h, act_l, first, last, kk=0, mt=2):
            wh, wl = unit(n)
            po = bank[b][:, :].rearrange("p (m s) -> p m s", m=2)
            tok = None
            for k in range(k0, k1):
                for m in range(mt):
                    end = last and k == k1 - 1
                    waits = [hi_t[n], lo_t[n], *ch_t(k + kk)] + (free[b] if first and k == k0 and m == 0 else [])
                    tok = three(po[:, m, :], wh[:, k, m * 128:(m + 1) * 128], wl[:, k, m * 128:(m + 1) * 128],
                                act_h[:, k + kk, :], act_l[:, k + kk, :],
                                start=(first and k == k0 and m == 0), stop=end,
                                tokens=waits, done=(k == k1 - 1 and m == mt - 1))
            return tok

        x_t = [None] * KD
        xs_t = [[None, None] for _ in range(KD)]

        def split_x(k, gain, gi):
            g = vcol(gain, gi)
            a = AC.do(lambda e: e.activation(xh[:, k, :], xT[:, k, :], ACT.Copy, scale=g), x_t[k], t_vec, PE.now())
            d = DV.do(lambda e: e.scalar_tensor_tensor(out=xl[:, k, :], in0=xT[:, k, :], scalar=g,
                                                       in1=xh[:, k, :].bitcast(F32), op0=ALU.mult,
                                                       op1=ALU.subtract), a)
            xs_t[k] = [a, d]

        ss_t = {"t": None}
        sq_free = {"t": None}

        def squares(c):
            if c == 0:
                ss_t["t"] = AC.do(lambda e: e.activation(ssum[:, :, :], xT[:, 0:2, :], ACT.Square),
                                  x_t[0], x_t[1], PE.now())
                return
            a = AC.do(lambda e: e.activation(sq[:, :, :], xT[:, 2 * c:2 * c + 2, :], ACT.Square),
                      x_t[2 * c], x_t[2 * c + 1], sq_free["t"])
            ss_t["t"] = sq_free["t"] = DV.do(
                lambda e: e.tensor_tensor(ssum[:, :, :], ssum[:, :, :], sq[:, :, :], ALU.add), a, ss_t["t"])

        ss2 = {"t": None, "sq": None}

        def scaled_squares(c):
            dst = ssum2 if c == 0 else sq2
            for m in range(2):
                a = AC.do(lambda e, m=m: e.activation(dst[:, m, :], xT[:, 2 * c + m, :], ACT.Square,
                                                      scale=vcol("norm_final", 2 * c + m)), x_t[2 * c + m],
                          ss2["sq"], t_vec)
            ss2["t"] = a if c == 0 else DV.do(lambda e: e.tensor_tensor(ssum2[:, :, :], ssum2[:, :, :], sq2[:, :, :],
                                                                        ALU.add), a, ss2["t"])
            ss2["sq"] = ss2["t"] if c else None

        def rsqrt(v, y, t, tok):
            tok = DV.do(lambda e: e.tensor_scalar(t.bitcast(I32), v.bitcast(I32), 1, None,
                                                  ALU.logical_shift_right), tok)
            tok = DV.do(lambda e: e.tensor_scalar(y.bitcast(I32), t.bitcast(I32), -1.0, MAGIC, ALU.mult,
                                                  ALU.add), tok)
            for _ in range(3):
                tok = DV.do(lambda e: e.scalar_tensor_tensor(out=t, in0=y, scalar=-0.5, in1=v, op0=ALU.mult,
                                                             op1=ALU.mult), tok)
                tok = DV.do(lambda e: e.tensor_tensor(t, t, y, ALU.mult), tok)
                tok = DV.do(lambda e: e.scalar_tensor_tensor(out=y, in0=t, scalar=1.5, in1=y, op0=ALU.add,
                                                             op1=ALU.mult), tok)
            return tok

        s_free, tb_free = {"t": []}, {"t": []}
        rcol, rv, rt = small[:, 0, 0:2], small[:, 1, 0:2], small[:, 2, 0:2]
        r_t = {"col": None, "row": None}

        def token_sums(src, dst, tok):
            for h in range(2):
                for c in range(2):
                    fn = lambda e, h=h, c=c: e.matmul(dst[:, h:h + 1], src[:, c, h * 128:(h + 1) * 128],
                                                      ones[:, 0:1], start=(h == 0 and c == 0), stop=(c == 1),
                                                      skip_group_check=True)
                    if h == 1 and c == 1:
                        return PE.do(fn)
                    PE.quiet(fn, tok, t_ones, *s_free["t"])

        def rms_col():
            m = token_sums(ssum, SB[:, 0, :], ss_t["t"])
            v = DV.do(lambda e: e.tensor_scalar(rv, SB[:, 0, 0:2], 1.0 / D, EPS, ALU.mult, ALU.add), m, AC.now(),
                      PE.now())
            s_free["t"] = [v]
            r_t["col"] = rsqrt(rv, rcol, rt, v)

        def rms_row(col=None, row=None, q=0):
            col = rcol if col is None else col
            row = rb if row is None else row
            for h in range(2):
                t = DV.do(lambda e, h=h: e.tensor_scalar(dg[:, h, :], ident, col[:, h:h + 1], None, ALU.mult),
                          r_t["col"], t_con, PE.now())
            PE.quiet(lambda e: e.matmul(TB[:, q, 0:128], ones[:, :], dg[:, 0, :], start=True, stop=True,
                                        skip_group_check=True), t, *tb_free["t"])
            m = PE.do(lambda e: e.matmul(TB[:, q, 128:256], ones[:, :], dg[:, 1, :], start=True, stop=True,
                                         skip_group_check=True))
            r_t["row"] = DV.do(lambda e: e.tensor_copy(row[:, :], TB[:, q, 0:256]), m)
            tb_free["t"] = [r_t["row"]]

        def residual(b, c, tok, gain=None, gi=0, sums=True):
            r = DV.do(lambda e: e.tensor_tensor(xT[:, 2 * c:2 * c + 2, :].rearrange("p k s -> p (k s)"),
                                                bank[b][:, :], xT[:, 2 * c:2 * c + 2, :].rearrange("p k s -> p (k s)"),
                                                ALU.add), tok, *xs_t[2 * c], *xs_t[2 * c + 1], AC.now())
            free[b] = [r]
            x_t[2 * c] = x_t[2 * c + 1] = r
            if sums:
                squares(c)
            if sums == 2:
                scaled_squares(c)
            if gain:
                for k in (2 * c, 2 * c + 1):
                    split_x(k, gain, gi + k)

        def ffn(layer, func, next_gain, next_gi, sums=True):
            cw = lambda tap, f: vcol("conv_w", (layer * 3 + tap) * NF + f)
            cb = lambda f: vcol("conv_b", layer * NF + f)
            late = []
            xw = lambda k: xs_t[k]
            for i in range(2):
                pads = DV.do(lambda e, i=i: e.memset(gp[i][:, :, 0:2], 0.0), PE.now(), AC.now())

            conv = [None, None]
            hs_t = [[None, None] for _ in range(NF)]

            def evacuate(i, bg, bu, tg, tu, top):
                g, ct, ub = gp[i % 2], cts[i % 2], ubs[i % 2]
                rbb = rb[:, :].unsqueeze(1).to_broadcast([128, 2, S])
                pg = bank[bg][:, :].rearrange("p (m s) -> p m s", m=2)
                pu = bank[bu][:, :].rearrange("p (m s) -> p m s", m=2)
                d0 = DV.do(lambda e: e.tensor_tensor(g[:, :, 2:S + 2], pg, rbb, ALU.mult), tg, r_t["row"], pads,
                           conv_read.get(i - 2))
                free[bg] = [d0]
                rest = late.pop(0)() if late else None
                a0 = AC.do(lambda e: e.activation(ct[:, 0, :], g[:, 0, 0:S], ACT.Identity, scale=cw(0, 2 * i),
                                                  bias=cb(2 * i)), d0)
                a1 = AC.do(lambda e: e.activation(ct[:, 1, :], g[:, 1, 0:S], ACT.Identity, scale=cw(0, 2 * i + 1),
                                                  bias=cb(2 * i + 1)), d0)
                if rest:
                    rest[0]()
                if stream["hi"] <= top:
                    split_hi()
                if stream["lo"] < stream["hi"] - 1:
                    split_lo()
                if rest:
                    rest[1]()
                d1 = DV.do(lambda e: e.tensor_tensor(ub[:, :, :], pu, rbb, ALU.mult), tu)
                free[bu] = [d1]
                for tap in (1, 2):
                    for m, a in ((0, a0), (1, a1)):
                        conv[m] = DV.do(lambda e, tap=tap, m=m: e.scalar_tensor_tensor(
                            out=ct[:, m, :], in0=g[:, m, tap:S + tap], scalar=cw(tap, 2 * i + m), in1=ct[:, m, :],
                            op0=ALU.mult, op1=ALU.add), a, conv[m])
                conv_read[i] = conv[1]
                if stream["hi"] <= top:
                    split_hi()
                if stream["lo"] < stream["hi"] - 1:
                    split_lo()
                a2 = AC.do(lambda e: e.activation(ct[:, :, :], ct[:, :, :], func), *conv)
                while stream["hi"] <= top and split_hi():
                    if stream["lo"] < stream["hi"] - 1:
                        split_lo()

                def finish():
                    d3 = DV.do(lambda e: e.tensor_tensor(hb[:, :, :], ct[:, :, :], ub[:, :, :], ALU.mult), a2, d1,
                               hs_t[2 * i - 1][0])
                    tk = {}

                    def high():
                        tk["a"] = AC.do(lambda e: e.activation(hh[:, 2 * i:2 * i + 2, :], hb[:, :, :], ACT.Copy), d3)

                    def low():
                        d4 = DV.do(lambda e: e.tensor_tensor(hl[:, 2 * i:2 * i + 2, :], hb[:, :, :],
                                                             hh[:, 2 * i:2 * i + 2, :].bitcast(F32), ALU.subtract),
                                   tk["a"])
                        hs_t[2 * i] = hs_t[2 * i + 1] = [tk["a"], d4]
                    return high, low
                late.append(finish)

            conv_read = {}
            for i in range(11):
                n0, n1_ = next_unit(), next_unit()
                ready(n1_)
                bg, bu = take(), take()
                if i == 0:
                    ready(n1_ + 2)
                    for k in range(KD):
                        tg = tensorT(n0, bg, k, k + 1, xw, xh, xl, k == 0, k == KD - 1)
                        tu = tensorT(n1_, bu, k, k + 1, xw, xh, xl, k == 0, k == KD - 1)
                        if k == KD - 1:
                            rms_col()
                    used[n0] = used[n1_] = tu
                    first = (i, bg, bu, tg, tu, n0 + 6)
                    continue
                else:
                    tg = used[n0] = tensorT(n0, bg, 0, KD, xw, xh, xl, True, True)
                    if i == 1:
                        rms_row()
                        evacuate(*first)
                    tu = used[n1_] = tensorT(n1_, bu, 0, KD, xw, xh, xl, True, True)
                evacuate(i, bg, bu, tg, tu, n0 + 6)
            for fn in late.pop(0)():
                fn()
            for c in range(4):
                b = take()
                k0 = 0
                for j, nk in enumerate((8, 8, 6)):
                    n = next_unit()
                    ahead(n)
                    t = used[n] = tensorT(n, b, 0, nk, lambda k: hs_t[k], hh, hl, j == 0, j == 2, kk=k0)
                    k0 += nk
                residual(b, c, t, next_gain, next_gi, sums)

        def natural(n, banks, act_h, act_l, act_t, halves=None):
            wh, wl = unit(n)
            _, _, nk, w = plan[n]
            toks = []
            for h in (range(2) if halves is None else halves):
                b = banks[h % len(banks)]
                po = bank[b][:, 0:w] if len(banks) == 2 else bank[b][:, h * 256:h * 256 + w]
                new = len(banks) == 2 or h == 0
                for k in range(nk):
                    waits = [hi_t[n], lo_t[n], *act_t(k)] + (free[b] if k == 0 and new else [])
                    sl = slice(h * 128, (h + 1) * 128)
                    tok = three(po, act_h[:, k, sl], act_l[:, k, sl], wh[:, k, :], wl[:, k, :],
                                start=(k == 0), stop=(k == nk - 1), tokens=waits, done=(k == nk - 1))
                toks.append(tok)
            return toks

        def stat(i, j):
            return small[:, 3 + i, 4 * (j % 3):4 * (j % 3) + 4]

        sc_free = [[], [], []]
        pt_t, o_t = {}, {}
        pt_free = {"t": []}
        p_t = {}
        v_t = {}

        def scores(j, heads, scale, mask, m_t):
            sc, mxs, nms, lsum = scs[j % 3], stat(0, j), stat(1, j), stat(2, j)
            for a, (q, k, toks) in enumerate(heads):
                PE.quiet(lambda e, a=a, q=q, k=k: e.matmul(SB[:, a, 0:128], q[:, 0:128], k[:, 0:128], start=True,
                                                           stop=True, skip_group_check=True), *toks, *s_free["t"])
                m = PE.do(lambda e, a=a, q=q, k=k: e.matmul(SB[:, a, 128:384], q[:, 128:256], k[:, 0:256],
                                                            start=True, stop=True, skip_group_check=True))
            d = DV.do(lambda e: e.scalar_tensor_tensor(out=sc[:, :, :], in0=SB[:, :, 0:384], scalar=scale, in1=mask,
                                                       op0=ALU.mult, op1=ALU.add), m, *m_t, *sc_free[j % 3])
            s_free["t"] = [d]
            d1 = DV.do(lambda e: e.tensor_reduce(mxs[:, 0:2], sc[:, :, 0:128], AX_X, ALU.max), d)
            d2 = DV.do(lambda e: e.tensor_reduce(mxs[:, 2:4], sc[:, :, 128:384], AX_X, ALU.max), d)
            d3 = DV.do(lambda e: e.tensor_scalar(nms, mxs, -1.0, None, ALU.mult), d1, d2)
            for a in range(2):
                for h, sl in ((0, slice(0, 128)), (1, slice(128, 384))):
                    x = AC.do(lambda e, a=a, h=h, sl=sl: e.activation(
                        sc[:, a, sl], sc[:, a, sl], ACT.Exp, bias=nms[:, 2 * h + a:2 * h + a + 1],
                        accum_out=lsum[:, 2 * h + a:2 * h + a + 1]), d3)
            p_t[j] = x

        def normalize(j):
            sc, lsum, linv = scs[j % 3], stat(2, j), stat(3, j)
            d = DV.do(lambda e: e.reciprocal(linv, lsum), p_t[j])
            for a in range(2):
                for h, sl in ((0, slice(0, 128)), (1, slice(128, 384))):
                    x = DV.do(lambda e, a=a, h=h, sl=sl: e.tensor_scalar(
                        sc[:, a, sl], sc[:, a, sl], linv[:, 2 * h + a:2 * h + a + 1], None, ALU.mult), d)
            p_t[j] = x

        def transposes(j):
            sc = scs[j % 3]
            for a in range(2):
                for c in range(3):
                    m = PE.do(lambda e, a=a, c=c: e.transpose(TB[:, a, c * 128:(c + 1) * 128],
                                                              sc[:, a, c * 128:(c + 1) * 128], ident),
                              p_t[j], *tb_free["t"])
            sc_free[j % 3] = [m]
            x = AC.do(lambda e: e.activation(pt[:, :, :], TB[:, :, 0:384], ACT.Copy), m, *pt_free["t"])
            tb_free["t"] = [x]
            pt_t[j] = x

        def values(j):
            b = take()
            for a in range(2):
                o = slice(64 * a, 64 * a + 64)
                col = slice((2 * j + a) * 64, (2 * j + a) * 64 + 64)
                PE.quiet(lambda e, a=a, o=o, col=col: e.matmul(bank[b][o, 0:128], vv[:, 0, col], pt[:, a, 0:128],
                                                               start=True, stop=True, skip_group_check=True),
                         pt_t[j], *v_t[j // 2], *free[b])
                PE.quiet(lambda e, a=a, o=o, col=col: e.matmul(bank[b][o, 128:256], vv[:, 0, col], pt[:, a, 128:256],
                                                               start=True, stop=False, skip_group_check=True))
                m = PE.do(lambda e, a=a, o=o, col=col: e.matmul(bank[b][o, 128:256], vv[:, 1, col],
                                                                pt[:, a, 256:384], start=False, stop=True,
                                                                skip_group_check=True))
            pt_free["t"] = [m]
            a_ = AC.do(lambda e: e.activation(oh[:, j, :], bank[b][:, 0:256], ACT.Copy), m)
            d_ = DV.do(lambda e: e.tensor_tensor(ol[:, j, :], bank[b][:, 0:256], oh[:, j, :].bitcast(F32),
                                                 ALU.subtract), a_)
            free[b] = [a_, d_]
            o_t[j] = [a_, d_]

        def project_out(gain, gi, sums=True):
            n0, n1_ = next_unit(), next_unit()
            bb = [None, None]
            st = {}
            ow = lambda k: o_t[k]

            def piece(ks):
                def run():
                    for k in ks:
                        if k == 0:
                            ahead(n0)
                            ahead(n1_)
                            st["b"] = (hold(), hold())
                        b0, b1 = st["b"]
                        st["t0"] = tensorT(n0, b0, k, k + 1, ow, oh, ol, k == 0, k == KD - 1)
                        st["t1"] = tensorT(n1_, b1, k, k + 1, ow, oh, ol, k == 0, k == KD - 1)
                return run

            def finish():
                used[n0] = used[n1_] = st["t1"]
                held.clear()
                ready(n0 + 5)
                for c in (2, 3):
                    n = next_unit()
                    b = take()
                    t = used[n] = tensorT(n, b, 0, KD, ow, oh, ol, True, True)
                    if c == 2:
                        residual(st["b"][0], 0, st["t1"], gain, gi, sums)
                        residual(st["b"][1], 1, st["t1"], gain, gi, sums)
                    residual(b, c, t, gain, gi, sums)

            return (lambda ks: piece(ks)()), finish

        def heads_mixer(kind, gain, gi):
            last = {}
            rc = {}

            def begin():
                rms_col()
                if kind == 0:
                    for h in range(2):
                        for nm, c in (("cos0", 0), ("sin0", 1)):
                            rc["t"] = DV.do(lambda e, h=h, nm=nm, c=c: e.tensor_scalar(
                                crs[:, c, h, :], cst(nm)[:, h * 64:(h + 1) * 64], rcol[:, h:h + 1], None, ALU.mult),
                                r_t["col"], t_con)

            def group(g):
                ns, st = {}, {}

                def half(part, h):
                    def run():
                        if h == 0:
                            ns[part] = next_unit()
                        n = ns[part]
                        if h == 0:
                            ahead(n)
                            st[part] = hold()
                        st[part, h] = natural(n, [st[part]], xh, xl, lambda k: xs_t[k], halves=[h])[0]
                        if h == 1:
                            used[n] = st[part, 1]
                            held.discard(st[part])
                            if g == 0 and part == 1:
                                begin()
                            evacuate(part)
                    return run

                def evacuate(part):
                    b, t = st[part], st[part, 1]
                    if part == 2:
                        for h in range(2):
                            a = AC.do(lambda e, h=h: e.activation(vv[:, h, g * 256:(g + 1) * 256],
                                                                  bank[b][:, h * 256:(h + 1) * 256], ACT.Copy,
                                                                  scale=rcol[:, h:h + 1]), t, r_t["col"])
                        free[b] = [a]
                        v_t[g] = [a]
                        return
                    dst = n1 if part == 0 else n2
                    flat = dst[:, :, 0:256]
                    if kind == 0:
                        tmp = rtmp
                        ps = bank[b][:, :].rearrange("p (t h d) -> p t h d", t=2, h=4)
                        fl = flat.rearrange("p t (h d) -> p t h d", h=4)
                        tm = tmp[:, :, 0:256].rearrange("p t (h d) -> p t h d", h=4)
                        wide = lambda c, lo, n: crs[:, c, :, lo:lo + n].unsqueeze(2).to_broadcast([128, 2, 4, n])
                        for q in range(2):
                            src = slice(32 - 32 * q, 64 - 32 * q)
                            d1 = DV.do(lambda e, q=q, src=src: e.tensor_tensor(
                                tm[:, :, :, 32 * q:32 * q + 32], ps[:, :, :, src], wide(1, 32 * q, 32), ALU.mult),
                                t, rc["t"], last.get("tmp"))
                        for h in range(2):
                            d0 = DV.do(lambda e, h=h: e.tensor_tensor(
                                fl[:, h], ps[:, h], crs[:, 0, h, :].unsqueeze(1).to_broadcast([128, 4, 64]),
                                ALU.mult), t, rc["t"], last.get(part))
                        free[b] = [d0, d1]
                        d = DV.do(lambda e: e.tensor_tensor(flat, flat, tmp[:, :, 0:256], ALU.add), d0, d1)
                        last["tmp"] = d
                        st["n", part] = d
                    else:
                        for h in range(2):
                            a = AC.do(lambda e, h=h: e.activation(flat[:, h, :], bank[b][:, h * 256:(h + 1) * 256],
                                                                  ACT.Copy, scale=rcol[:, h:h + 1]),
                                      t, r_t["col"], last.get(part))
                        free[b] = [a]
                        x = AC.do(lambda e: e.activation(rtmp[:, :, 0:256], flat, ACT.Square), a, last.get("tmp"))
                        ss = small[:, 7, 0:8]
                        vs = small[:, 8, 0:8]
                        ys = small[:, 9 + part, 0:8]
                        tt = small[:, 11, 0:8]
                        d = DV.do(lambda e: e.tensor_reduce(
                            ss.rearrange("p (t h) -> p t h", t=2),
                            rtmp[:, :, 0:256].rearrange("p t (h d) -> p t h d", h=4), AX_X, ALU.add), x)
                        last["tmp"] = d
                        d = DV.do(lambda e: e.tensor_scalar(vs, ss, 1.0 / 64, EPS, ALU.mult, ALU.add), d)
                        d = rsqrt(vs, ys, tt, d)
                        for h in range(2):
                            f4 = flat[:, h, :].rearrange("p (h d) -> p h d", h=4)
                            st["n", part] = DV.do(lambda e, h=h, f4=f4: e.tensor_tensor(
                                f4, f4, ys[:, 4 * h:4 * h + 4].unsqueeze(2).to_broadcast([128, 4, 64]), ALU.mult), d)

                def turn_over(part):
                    def run():
                        src = n1 if part == 0 else n2
                        dst = (qT if part == 0 else kT)[g % 2]
                        b = take()
                        for c in range(2):
                            for h in range(2):
                                m = PE.do(lambda e, c=c, h=h: e.transpose(
                                    bank[b][:, c * 256 + h * 128:c * 256 + (h + 1) * 128],
                                    src[:, h, c * 128:(c + 1) * 128], ident), st["n", part], t_con, *free[b])
                        last[part] = m
                        kw = {"scale": vcol("q_norm" if part == 0 else "k_norm", 0)} if kind == 3 else {}
                        a = AC.do(lambda e: e.activation(dst[:, :, :].rearrange("p c s -> p (c s)"), bank[b][:, :],
                                                         ACT.Copy, **kw), m, PE.now())
                        free[b] = [a]
                        tt_t[g, part] = a
                    return run

                def bias():
                    if kind == 3:
                        load = (s_bias[0], 16 * (g + 1))
                        SP.wait(bw_free["t"], bm_t.get(g - 1))
                        SP.quiet(lambda e: e.dma_start(bw[0][:, :, :], dram["bias"][g]).then_inc(s_bias[0], 16))
                        m3 = cst("mask3")
                        p0 = PO.do(lambda e: e.tensor_tensor(
                            bm[g % 2][:, :, 0:128], bw[0][:, :, 128:256],
                            m3[:, 0:128].unsqueeze(1).to_broadcast([128, 4, 128]), ALU.add),
                            load, t_con, sc_read[g - 2] if g >= 2 else None)
                        p1 = PO.do(lambda e: e.tensor_tensor(
                            bm[g % 2][:, :, 128:384], bw[0][:, :, :],
                            m3[:, 128:384].unsqueeze(1).to_broadcast([128, 4, 256]), ALU.add))
                        bm_t[g] = p1
                bias()
                return half, turn_over

            tt_t, bm_t, sc_read = {}, {}, {}
            bw_free = {"t": PE.now()}

            def pair_heads(j):
                g, c = j // 2, j % 2
                tk = [tt_t[g, 0], tt_t[g, 1]]
                return [(qT[g % 2][64 * a:64 * a + 64, c, :], kT[g % 2][64 * a:64 * a + 64, c, :], tk)
                        for a in range(2)]

            def mask_of(j):
                if kind == 0:
                    return cst("mask0").unsqueeze(1).to_broadcast([128, 2, 384]), [t_con]
                g, c = j // 2, j % 2
                return bm[g % 2][:, 2 * c:2 * c + 2, :], [bm_t[g]]

            groups = {0: group(0)}
            half, turn_over = groups[0]
            for p in (half(1, 0), half(1, 1), half(0, 0), half(0, 1), turn_over(1), turn_over(0)):
                p()

            def slots_of(g):
                v = groups[g][0]
                if g == 3:
                    return [[v(2, 0)], [v(2, 1)], []]
                half, turn_over = groups[g + 1] = group(g + 1)
                return [[half(1, 0)], [half(1, 1)], [half(0, 0)], [half(0, 1), turn_over(1)], [v(2, 0)],
                        [turn_over(0), v(2, 1)]]

            sc_free[0] = sc_free[1] = sc_free[2] = [PE.now()]
            weave(slots_of, pair_heads, 0.125, mask_of, gain, gi, sc_read)

        def weave(slots_of, pair_heads, scale, mask_of, gain, gi, sc_read):
            def run(pieces):
                for p in pieces:
                    p()

            def step(j, slots):
                if j >= 1:
                    normalize(j - 1)
                if len(slots) > 3:
                    run(slots[3])
                scores(j, pair_heads(j), scale, *mask_of(j))
                run(slots[0])
                if j >= 2:
                    transposes(j - 2)
                catch_up()
                run(slots[1])
                if j >= 2:
                    values(j - 2)
                catch_up()
                run(slots[2])

            lazy["on"], lazy["n"] = True, at["unit"] - 1
            for g in range(3):
                slots = slots_of(g)
                step(2 * g, slots[0:3])
                step(2 * g + 1, slots[3:])
                sc_read[g] = DV.now()
            slots = slots_of(3)
            step(6, slots[0:3])
            wo, finish = project_out(gain, gi)
            step(7, [[lambda: wo([0, 1])], [lambda: wo([2, 3])], [lambda: wo([4])]])
            normalize(7)
            transposes(6)
            wo([5])
            values(6)
            transposes(7)
            catch_up()
            wo([6])
            values(7)
            wo([7])
            lazy["on"] = False
            finish()

        def latent_mixer(gain, gi):
            tcol = small[:, 12, 0:4]
            c_t = {}
            banks_of = {}
            ns = [next_unit() for _ in range(3)]
            ahead(ns[0])
            for i, n in enumerate(ns):
                ahead(n)
                w = plan[n][3]
                b = take()
                t = used[n] = natural(n, [b], xh, xl, lambda k: xs_t[k])[-1]
                if i == 0:
                    rms_col()
                for h in range(2):
                    a = AC.do(lambda e, h=h, b=b, i=i, w=w: e.activation(
                        cc[:, h, i * 256:i * 256 + w], bank[b][:, h * 256:h * 256 + w], ACT.Copy,
                        scale=rcol[:, h:h + 1]), t, r_t["col"])
                free[b] = [a]
                c_t[i] = a
                if i:
                    latent_chunks(c_t[i - 1], (0, 1) if i == 1 else (2, 3))
            latent_chunks(c_t[2], (4,))
            lv, ly, lt = small[:, 13, 0:4], small[:, 14, 0:4], small[:, 15, 0:4]
            for h in range(2):
                AC.do(lambda e, h=h: e.activation(n1[:, 0, 0:384], cc[:, h, 0:384], ACT.Square,
                                                  accum_out=tcol[:, h:h + 1]), c_t[2], AC.now())
                a = AC.do(lambda e, h=h: e.activation(n1[:, 1, 0:256], cc[:, h, 384:640], ACT.Square,
                                                      accum_out=tcol[:, 2 + h:3 + h]), AC.now())
            d = DV.do(lambda e: e.tensor_scalar(lv[:, 0:2], tcol[:, 0:2], 1.0 / 384, EPS, ALU.mult, ALU.add), a)
            d = DV.do(lambda e: e.tensor_scalar(lv[:, 2:4], tcol[:, 2:4], 1.0 / 256, EPS, ALU.mult, ALU.add), a)
            l_t = rsqrt(lv, ly, lt, d)
            cs, sn = (cst(x).rearrange("p (t d) -> p t d", t=2) for x in ("cos1", "sin1"))
            krs = cc[:, :, 640:672]
            d = DV.do(lambda e: e.tensor_tensor(kr[:, :, :], krs, cs, ALU.mult), c_t[2], t_con)
            tmp = rtmp[:, :, 0:32]
            d1 = DV.do(lambda e: e.tensor_tensor(tmp[:, :, 0:16], krs[:, :, 16:32], sn[:, :, 0:16], ALU.mult))
            d1 = DV.do(lambda e: e.tensor_tensor(tmp[:, :, 16:32], krs[:, :, 0:16], sn[:, :, 16:32], ALU.mult))
            kr_t = DV.do(lambda e: e.tensor_tensor(kr[:, :, :], kr[:, :, :], tmp, ALU.add), d, d1)
            kr_p = PO
            last = {}
            tt_t = {}

            def group(g):
                nq, nkv = next_unit(), next_unit()
                st = {}

                def q_half(h):
                    def run():
                        if h == 0:
                            ahead(nq)
                        b = take()
                        t = natural(nq, [b, b], ch, cl, lambda k: cs_t[k], halves=[h])[0]
                        if h == 1:
                            used[nq] = t
                        a = AC.do(lambda e: e.activation(n1[:, h, :], bank[b][:, 0:384], ACT.Copy,
                                                         scale=ly[:, h:h + 1]), t, l_t, last.get("q"))
                        free[b] = [a]
                        if h == 1:
                            nr = n1[:, :, :].rearrange("p t (h d) -> p t h d", h=4)[:, :, :, 64:96]
                            tm = rtmp[:, :, 0:128].rearrange("p t (h d) -> p t h d", h=4)
                            wide = lambda x, lo, n: x[:, :, lo:lo + n].unsqueeze(2).to_broadcast([128, 2, 4, n])
                            d1 = DV.do(lambda e: e.tensor_tensor(tm[:, :, :, 0:16], nr[:, :, :, 16:32],
                                                                 wide(sn, 0, 16), ALU.mult), a, DV.now())
                            d1 = DV.do(lambda e: e.tensor_tensor(tm[:, :, :, 16:32], nr[:, :, :, 0:16],
                                                                 wide(sn, 16, 16), ALU.mult))
                            for tt in range(2):
                                d0 = DV.do(lambda e, tt=tt: e.tensor_tensor(
                                    nr[:, tt], nr[:, tt], cs[:, tt, :].unsqueeze(1).to_broadcast([128, 4, 32]),
                                    ALU.mult), d1)
                            for tt in range(2):
                                d = DV.do(lambda e, tt=tt: e.tensor_tensor(nr[:, tt], nr[:, tt], tm[:, tt],
                                                                           ALU.add), d0, d1)
                            st["q"] = d
                    return run

                def kv_half(h):
                    def run():
                        if h == 0:
                            ahead(nkv)
                        b = take()
                        t = natural(nkv, [b, b], ch[:, 3:5, :], cl[:, 3:5, :], lambda k: cs_t[3 + k], halves=[h])[0]
                        if h == 1:
                            used[nkv] = t
                        pv = bank[b][:, :].rearrange("p (h d) -> p h d", h=4)
                        k4 = n2[:, h, :].rearrange("p (h d) -> p h d", h=4)
                        d = DV.do(lambda e: e.tensor_scalar(k4[:, :, 0:64], pv[:, :, 0:64], ly[:, 2 + h:3 + h],
                                                            None, ALU.mult), t, l_t, last.get("k"))
                        a = AC.do(lambda e: e.activation(
                            vv[:, h, g * 256:(g + 1) * 256].rearrange("p (h d) -> p h d", h=4), pv[:, :, 64:128],
                            ACT.Copy, scale=ly[:, 2 + h:3 + h]), t, l_t, d)
                        free[b] = [a]
                        p = PO.do(lambda e: e.tensor_copy(k4[:, :, 64:96],
                                                          kr[:, h, :].unsqueeze(1).to_broadcast([128, 4, 32])),
                                  kr_t, last.get("k"))
                        st["k", h] = [d, p]
                        v_t[g] = [a]
                    return run

                def turn_over(part, c):
                    def run():
                        src = n1 if part == 0 else n2
                        dst = (qM if part == 0 else kM)[g % 2]
                        b = take()
                        toks = [st["q"]] if part == 0 else st["k", 0] + st["k", 1]
                        for a_ in range(2):
                            for h in range(2):
                                hd = 2 * c + a_
                                m = PE.do(lambda e, a_=a_, h=h, hd=hd: e.transpose(
                                    bank[b][0:96, a_ * 256 + h * 128:a_ * 256 + (h + 1) * 128],
                                    src[:, h, hd * 96:(hd + 1) * 96], ident), *toks, t_con, *free[b])
                        last["q" if part == 0 else "k"] = m
                        flat = dst[:, 2 * c:2 * c + 2, :].rearrange("p c s -> p (c s)")
                        if part == 0:
                            a = AC.do(lambda e: e.activation(flat, bank[b][0:96, :], ACT.Copy), m, PE.now())
                        else:
                            a = DV.do(lambda e: e.tensor_copy(flat, bank[b][0:96, :]), m, PE.now())
                        free[b] = [a]
                        tt_t[g, part, c] = a
                    return run
                return [[q_half(0), q_half(1)], [kv_half(0)], [kv_half(1)], [], [], [],
                        [turn_over(0, 0), turn_over(0, 1), turn_over(1, 0), turn_over(1, 1)]]

            def pair_heads(j):
                g, c = j // 2, j % 2
                tk = [tt_t[g, 0, c], tt_t[g, 1, c]]
                return [(qM[g % 2][:, 2 * c + a, :], kM[g % 2][:, 2 * c + a, :], tk) for a in range(2)]

            mask_of = lambda j: (cst("mask0").unsqueeze(1).to_broadcast([128, 2, 384]), [t_con])
            for p in sum(group(0), []):
                p()
            slots_of = lambda g: group(g + 1) if g < 3 else [[], [], []]
            weave(slots_of, pair_heads, 96 ** -0.5, mask_of, gain, gi, {})

        cs_t = {}

        def latent_chunks(tok, chunks):
            for c in chunks:
                b = take()
                for h in range(2):
                    m = PE.do(lambda e, h=h, c=c, b=b: e.transpose(bank[b][:, h * 128:(h + 1) * 128],
                                                                   cc[:, h, c * 128:(c + 1) * 128], ident),
                              tok, t_con, *free[b])
                g = vcol("b_q_norm", c) if c < 3 else vcol("b_kv_norm", c - 3)
                a = AC.do(lambda e, c=c, b=b, g=g: e.activation(ch[:, c, :], bank[b][:, 0:256], ACT.Copy, scale=g), m)
                d = DV.do(lambda e, c=c, b=b, g=g: e.scalar_tensor_tensor(
                    out=cl[:, c, :], in0=bank[b][:, 0:256], scalar=g, in1=ch[:, c, :].bitcast(F32), op0=ALU.mult,
                    op1=ALU.subtract), a)
                free[b] = [a, d]
                cs_t[c] = [a, d]

        def pool_mixer(next_gain, next_gi):
            n = next_unit()
            ready(n)
            t1 = token_sums(ssum, SB[:, 0, :], ss_t["t"])
            t2 = token_sums(ssum2, SB[:, 1, :], ss2["t"])
            z = PO.do(lambda e: e.memset(ph[:, :, 0:16], 0.0), PE.now(), AC.now(), DV.now())
            for i in range(5):
                z = PO.do(lambda e, i=i: e.memset(pa[i][:, :, 0:16], 0.0))
            gg, r2, rr = small[:, 4, 0:8], small[:, 5, 0:2], small[:, 6, 0:2]
            v = lambda name: vec[:, VEC_AT[name]:VEC_AT[name] + 8]
            t_gg = DV.do(lambda e: e.tensor_tensor(gg, v("norm_final"), v("mix_norm_2"), ALU.mult), t_vec, PE.now(),
                         AC.now())
            bs = small[:, 3, 0:8]
            t_bs = DV.do(lambda e: e.tensor_tensor(bs, v("pool_b"), v("pool_scale"), ALU.mult))
            t = DV.do(lambda e: e.tensor_scalar(rv, SB[:, 0, 0:2], 1.0 / D, EPS, ALU.mult, ALU.add), t1)
            t = rsqrt(rv, rcol, rt, t)
            t = DV.do(lambda e: e.tensor_tensor(rv, rcol, rcol, ALU.mult), t)
            t = DV.do(lambda e: e.tensor_tensor(rv, rv, SB[:, 1, 0:2], ALU.mult), t, t2)
            t = DV.do(lambda e: e.tensor_scalar(rv, rv, 1.0 / D, EPS, ALU.mult, ALU.add), t)
            s_free["t"] = [t]
            t = rsqrt(rv, r2, rt, t)
            r_t["col"] = DV.do(lambda e: e.tensor_tensor(rr, rcol, r2, ALU.mult), t)
            rms_row(rr, rb2, 0)
            t_both = r_t["row"]
            rms_row(rcol, rb, 1)
            order = (3, 1, 0, 2)
            h_t, y_t, xn_t = {}, {}, {}
            icnt = cst("icnt").rearrange("p (g s) -> p g s", g=4)

            bufs_of = {1: pa[0:2], 0: pa[2:3], 3: pa[3:5], 2: pa[3:5]}

            def normed(g):
                for k in (2 * g, 2 * g + 1):
                    h_t[g] = DV.do(lambda e, k=k: e.scalar_tensor_tensor(
                        out=ph[:, k, 16:S + 16], in0=xT[:, k, :], scalar=gg[:, k:k + 1], in1=rb2[:, :],
                        op0=ALU.mult, op1=ALU.mult), x_t[k], t_both, t_gg, PE.now())

            def windows(g):
                E = PO if g < 2 else DV
                h = ph[:, 2 * g:2 * g + 2, :]
                src, bufs = h, bufs_of[g]
                tok = h_t[g]
                for lvl in range(g + 1):
                    sh = 1 << lvl
                    dst = bufs[lvl % 2]
                    tok = E.do(lambda e, src=src, dst=dst, sh=sh: e.tensor_tensor(
                        dst[:, :, 16:S + 16], src[:, :, 16:S + 16], src[:, :, 16 - sh:S + 16 - sh], ALU.add),
                        tok, z, E.now())
                    src = dst
                return src, tok

            def differences(g, src, tok):
                h, f, w = ph[:, 2 * g:2 * g + 2, :], fix[g], 2 << g
                t0 = DV.do(lambda e: e.tensor_tensor(f[:, :, :], src[:, :, 16:32],
                                                    icnt[:, g, :].unsqueeze(1).to_broadcast([128, 2, 16]), ALU.mult),
                          tok, t_con)
                t0 = DV.do(lambda e: e.tensor_tensor(f[:, :, :], f[:, :, :], h[:, :, 16:32], ALU.subtract), t0)
                t1 = DV.do(lambda e: e.scalar_tensor_tensor(
                    out=h[:, :, 16:S + 16], in0=src[:, :, 16:S + 16], scalar=1.0 / w, in1=h[:, :, 16:S + 16],
                    op0=ALU.mult, op1=ALU.subtract), t0)
                y_t[g] = DV.do(lambda e: e.tensor_copy(h[:, :, 16:32], f[:, :, :]), t1)

            normed(1)
            normed(0)
            normed(3)
            w1, w0, w3 = windows(1), windows(0), windows(3)
            differences(3, *w3)
            differences(1, *w1)
            normed(2)
            differences(0, *w0)
            differences(2, *windows(2))
            wh, wl = unit(n)
            for g in order:
                a = AC.do(lambda e, g=g: e.activation(xh[:, 2 * g:2 * g + 2, :], ph[:, 2 * g:2 * g + 2, 16:S + 16],
                                                      ACT.Copy), y_t[g], PE.now())
                d = DV.do(lambda e, g=g: e.tensor_tensor(xl[:, 2 * g:2 * g + 2, :], ph[:, 2 * g:2 * g + 2, 16:S + 16],
                                                         xh[:, 2 * g:2 * g + 2, :].bitcast(F32), ALU.subtract), a)
                for k in (2 * g, 2 * g + 1):
                    xs_t[k] = [a, d]
            ready(n + 2)
            for k in range(KD):
                x_t[k] = DV.do(lambda e, k=k: e.scalar_tensor_tensor(
                    out=xT[:, k, :], in0=xT[:, k, :], scalar=vcol("norm_final", k), in1=rb[:, :], op0=ALU.mult,
                    op1=ALU.mult), r_t["row"], x_t[k], AC.now())
                x_t[k] = DV.do(lambda e, k=k: e.tensor_scalar(xT[:, k, :], xT[:, k, :], bs[:, k:k + 1], None,
                                                              ALU.add), t_bs, x_t[k])
            done_t = []
            for g in order:
                b = take()
                for k in (0, 1):
                    for m in range(2):
                        t = three(bank[b][:, m * 256:(m + 1) * 256], wh[:, 2 * g + k, m * 128:(m + 1) * 128],
                                  wl[:, 2 * g + k, m * 128:(m + 1) * 128], xh[:, 2 * g + k, :], xl[:, 2 * g + k, :],
                                  start=(k == 0 and m == 0), stop=(k == 1),
                                  tokens=[hi_t[n], lo_t[n], *xs_t[2 * g + k], *free[b]], done=(k == 1 and m == 1))
                done_t.append((g, b, t))
            used[n] = t
            for g, b, t in done_t:
                for m in range(2):
                    k = 2 * g + m
                    d = DV.do(lambda e, k=k, m=m, b=b: e.scalar_tensor_tensor(
                        out=xT[:, k, :], in0=bank[b][:, m * 256:(m + 1) * 256], scalar=vcol("pool_scale", k),
                        in1=xT[:, k, :], op0=ALU.mult, op1=ALU.add), t, x_t[k])
                    x_t[k] = d
                free[b] = [d]
            for c in range(4):
                squares(c)
                for k in (2 * c, 2 * c + 1):
                    split_x(k, next_gain, next_gi + k)

        load_unit()
        SP.quiet(lambda e: e.dma_start(xT[:, 4:8, :], dram["x"][:, 4:8, :]).then_inc(s_x2, 16))
        load_unit()
        load_unit()
        SP.quiet(lambda e: e.dma_start(con[:, :], dram["con"]).then_inc(s_con, 16))
        for k in range(KD):
            x_t[k] = t_x if k < 4 else t_x2
        for k in range(4):
            split_x(k, "norm_mix", k)
        ready(0)
        for k in range(4, KD):
            split_x(k, "norm_mix", k)
        ready(1)
        for c in range(4):
            squares(c)
        heads_mixer(0, "norm_ffn", 0)
        ffn(0, ACT.Gelu, "norm_mix", 8)
        latent_mixer("norm_ffn", 8)
        ffn(1, ACT.Gelu, None, 0, sums=2)
        pool_mixer("ffn_norm_2", 0)
        ffn(2, ACT.Silu, "mix_norm_2", 8)
        heads_mixer(3, "ffn_norm_2", 8)
        ffn(3, ACT.Silu, None, 0)
        SP.wait(*x_t)
        SP.quiet(lambda e: e.dma_start(out, xT[:, :, :]).then_inc(s_out, 16))
        SP.quiet(lambda e: e.wait_ge(s_out, 16))

        block = ctx.enter_context(nc.Block())

        @block.sync
        def _(e):
            SP.play(e)

        @block.scalar
        def _(e):
            AC.play(e)

        @block.vector
        def _(e):
            DV.play(e)

        @block.gpsimd
        def _(e):
            PO.play(e)

        @block.tensor
        def _(e):
            PE.play(e)


def lay_units(w, cols, nk=None):
    k, n = w.shape
    v = w.reshape(k // 128, 128, n // cols, cols)
    return np.ascontiguousarray(v.transpose(2, 1, 0, 3)).reshape(n // cols, 128, k // 128 * cols)


def chan(v):
    return np.ascontiguousarray(v.reshape(-1, 128).T)


def constants():
    def rope(dim):
        inv = np.float32(10000.0) ** (-np.arange(0, dim, 2, dtype=np.float32) / np.float32(dim))
        ang = np.arange(S, dtype=np.float32)[:, None] * inv[None, :].astype(np.float32)
        c, s = np.cos(ang).astype(np.float32), np.sin(ang).astype(np.float32)
        lay = lambda a: a.reshape(2, 128, dim).transpose(1, 0, 2).reshape(128, 2 * dim)
        return lay(np.concatenate([c, c], 1)), lay(np.concatenate([-s, s], 1))

    p = np.arange(128)[:, None]
    c0, s0 = rope(64)
    c1, s1 = rope(32)
    k0, k1 = np.arange(128)[None, :], np.arange(256)[None, :]
    big = np.float32(-1e30)
    mask0 = np.concatenate([np.where(k0 <= p, 0, big), np.where(k1 <= p + 128, 0, big)], 1)
    mask3 = np.concatenate([np.where(k0 // 64 <= p // 64, 0, big),
                            np.where(k1 // 64 <= (p + 128) // 64, 0, big)], 1)
    icnt = np.concatenate([1.0 / np.minimum(np.arange(16) + 1, w) for w in (2, 4, 8, 16)])[None].repeat(128, 0)
    return np.ascontiguousarray(np.concatenate([np.eye(128), c0, s0, c1, s1, mask0, mask3, icnt], 1),
                                dtype=np.float32)


def kernel(**inputs):
    import concourse.bacc as _bacc
    from concourse.bass_utils import run_bass_kernel_spmd as _run

    i = {k: np.asarray(v) for k, v in inputs.items()}
    a = {}
    a["x"] = i["x"][0].T.reshape(KD, 128, S).transpose(1, 0, 2)
    a["con"] = constants()
    a["vec"] = np.concatenate([
        chan(i["norm_mix"]), chan(i["norm_ffn"]), chan(i["norm_final"]), chan(i["mix_norm_2"]),
        chan(i["ffn_norm_2"]), chan(i["pool_b_2"]), chan(i["pool_scale_2"]), chan(i["b_q_norm"]),
        chan(i["b_kv_norm"]), chan(np.concatenate([i["attn_q_norm_2"], i["attn_q_norm_2"]], 1)),
        chan(np.concatenate([i["attn_k_norm_2"], i["attn_k_norm_2"]], 1)),
        chan(i["ffn_conv_w"]), chan(i["ffn_conv_w_2"]), chan(i["ffn_conv_b"]), chan(i["ffn_conv_b_2"])], 1)
    a["a_qkv"] = lay_units(i["a_w_qkv"][0], 256)
    a["a_o"] = lay_units(i["a_w_o"][0], 256)
    a["b_in"] = lay_units(i["b_w_in"][0][:, 0:512], 256)
    a["b_in2"] = lay_units(i["b_w_in"][0][:, 512:672], 160)
    a["b_uq"] = lay_units(i["b_w_uq"][0], 384)
    a["b_ukv"] = lay_units(i["b_w_ukv"][0], 512)
    a["b_o"] = lay_units(i["b_w_o"][0], 256)
    a["pool"] = i["pool_w_2"][0].reshape(8, 128, 256).transpose(1, 0, 2).reshape(1, 128, 2048)
    a["d_qkv"] = lay_units(i["attn_wqkv_2"][0], 256)
    a["d_o"] = lay_units(i["attn_wo_2"][0], 256)
    for layer in range(4):
        j = layer % 2
        g, u, d = (("ffn_w_gate", "ffn_w_up", "ffn_w_down"), ("ffn_w_gate_2", "ffn_w_val_2", "ffn_w_out_2"))[
            layer // 2]
        a[f"gate{layer}"] = lay_units(i[g][j], 256)
        a[f"up{layer}"] = lay_units(i[u][j], 256)
        for c, (k0, k1) in enumerate(((0, 1024), (1024, 2048), (2048, 2816))):
            a[f"down{layer}_{c}"] = lay_units(i[d][j][k0:k1], 256)
    idx = 384 + np.arange(128)[:, None] - np.arange(256)[None, :]
    a["bias"] = i["attn_rel_bias_2"][0][:, idx].reshape(4, 4, 128, 256).transpose(0, 2, 1, 3)
    a = {k: np.ascontiguousarray(v, dtype=v.dtype) for k, v in a.items()}

    nc = _bacc.Bacc("TRN2", target_bir_lowering=False, num_devices=1, dynamic_dma_scratch_size=1024)
    dram = {k: nc.dram_tensor(f"in_{k}", v.shape, mybir.dt.from_np(v.dtype), kind="ExternalInput").ap()
            for k, v in a.items()}
    out = nc.dram_tensor("out_0", (128, KD, S), F32, kind="ExternalOutput").ap()
    build(nc, dram, out)
    r = _run(nc, [{f"in_{k}": v for k, v in a.items()}], core_ids=[0])
    got = r.results[0]["out_0"]
    return np.ascontiguousarray(got.transpose(1, 0, 2).reshape(D, S).T).reshape(1, S, D)
```

```python
from contextlib import ExitStack

import numpy as np

import concourse.bass as bass
from concourse import mybir

F32 = mybir.dt.float32
F32R = mybir.dt.float32r
I32 = mybir.dt.int32
ALU = mybir.AluOpType
ACT = mybir.ActivationFunctionType
AX_X = mybir.AxisListType.X

S, D, KD = 256, 1024, 8
NF = 22
NG = 4
UNIT = 2048
RAW, RING = 3, 5
LOOK = 2
EPS = 1e-6
MAGIC = 1597463007.0

VECS = [("norm_mix", 16), ("norm_ffn", 16), ("norm_final", 8), ("mix_norm_2", 16), ("ffn_norm_2", 16),
        ("pool_b", 8), ("pool_scale", 8), ("b_q_norm", 3), ("b_kv_norm", 2), ("q_norm", 1), ("k_norm", 1),
        ("conv_w", 4 * 3 * NF), ("conv_b", 4 * NF)]
VEC_AT, VEC_N = {}, 0
for _name, _n in VECS:
    VEC_AT[_name] = VEC_N
    VEC_N += _n

CONSTS = [("ident", 128), ("cos0", 128), ("sin0", 128), ("cos1", 64), ("sin1", 64), ("mask0", 384),
          ("mask3", 384)]
CON_AT, CON_N = {}, 0
for _name, _n in CONSTS:
    CON_AT[_name] = CON_N
    CON_N += _n


def unit_plan():
    plan = []

    def qkv(name):
        unit = lambda part, g: plan.append((name, part * 4 + g, KD, 256))
        for g in range(4):
            for part in (1, 0, 2):
                unit(part, g)

    def out(name):
        for m in range(4):
            plan.append((name, m, KD, 256))

    def ffn(layer):
        for i in range(11):
            plan.append((f"gate{layer}", i, KD, 256))
            plan.append((f"up{layer}", i, KD, 256))
        for m in range(4):
            for c, nk in enumerate((8, 8, 6)):
                plan.append((f"down{layer}_{c}", m, nk, 256))

    qkv("a_qkv")
    out("a_o")
    ffn(0)
    plan.append(("b_in", 0, KD, 256))
    plan.append(("b_in", 1, KD, 256))
    plan.append(("b_in2", 0, KD, 160))
    for g in range(4):
        plan.append(("b_uq", g, 3, 384))
        plan.append(("b_ukv", g, 2, 512))
    out("b_o")
    ffn(1)
    plan.append(("pool", 0, KD, 256))
    ffn(2)
    qkv("d_qkv")
    out("d_o")
    ffn(3)
    return plan


class Engine:

    def __init__(self, name, sem):
        self.name, self.sem, self.n, self.queue, self.seen = name, sem, 0, [], {}

    def wait(self, *tokens):
        for t in tokens:
            if t is None:
                continue
            sem, value = t
            if self.seen.get(id(sem), 0) < value:
                self.seen[id(sem)] = value
                self.queue.append(lambda e, sem=sem, value=value: e.wait_ge(sem, value))

    def do(self, fn, *tokens):
        self.wait(*tokens)
        self.n += 1
        self.queue.append(lambda e: fn(e).then_inc(self.sem, 1))
        return (self.sem, self.n)

    def quiet(self, fn, *tokens):
        self.wait(*tokens)
        self.queue.append(fn)

    def now(self):
        return (self.sem, self.n)

    def play(self, e):
        for fn in self.queue:
            fn(e)


def build(nc, dram, out):
    plan = unit_plan()
    with ExitStack() as ctx:
        def sb(name, shape, dt=F32, stack=ctx):
            return stack.enter_context(nc.sbuf_tensor(name, shape, dt))

        def sem(name):
            return ctx.enter_context(nc.semaphore(name))

        PE = Engine("pe", sem("s_pe"))
        AC = Engine("act", sem("s_act"))
        DV = Engine("dve", sem("s_dve"))
        PO = Engine("pool", sem("s_pool"))
        SP = Engine("sp", sem("s_sp"))
        s_raw = [sem(f"s_raw{i}") for i in range(RAW)]
        s_con, s_x, s_vec, s_out, s_x2, s_win = (sem(f"s_{x}") for x in ("con", "x", "vec", "out", "x2", "win"))
        s_bias = [sem("s_bias0"), sem("s_bias1")]

        raw = [sb(f"raw{i}", [128, UNIT]) for i in range(RAW)]
        whi = [sb(f"whi{i}", [128, UNIT], F32R) for i in range(RING)]
        wlo = [sb(f"wlo{i}", [128, UNIT], F32R) for i in range(RING)]
        xT = sb("xT", [128, KD, S])
        xh = sb("xh", [128, KD, S], F32R)
        xl = sb("xl", [128, KD, S], F32R)
        con = sb("con", [128, CON_N])
        vec = sb("vec", [128, VEC_N])
        ones = sb("ones", [128, 128])
        sq = sb("sq", [128, 2, S])
        ssum = sb("ssum", [128, 2, S])
        rb = sb("rb", [128, S])
        small = sb("small", [128, 16, 16])

        dg = sb("dg", [128, 2, 128])
        crs = sb("crs", [128, 2, 2, 64])
        rtmp = sb("rtmp", [128, 2, 256])

        ffn_mem = ExitStack()
        hh = sb("hh", [128, NF, S], F32R, ffn_mem)
        hl = sb("hl", [128, NF, S], F32R, ffn_mem)
        gp = [sb(f"gp{i}", [128, 2, S + 2], F32, ffn_mem) for i in range(2)]
        ssum2 = sb("ssum2", [128, 2, S], F32, ffn_mem)
        sq2 = sb("sq2", [128, 2, S], F32, ffn_mem)
        cts = [sb(f"ct{i}", [128, 2, S], F32, ffn_mem) for i in range(2)]
        ubs = [sb(f"ub{i}", [128, 2, S], F32, ffn_mem) for i in range(2)]
        hb = sb("hb", [128, 2, S], F32, ffn_mem)
        wins = sb("wins", [128, NG, 384], F32, ffn_mem)
        ffn_mem.close()

        att_mem = ExitStack()
        oh = sb("oh", [128, KD, S], F32R, att_mem)
        ol = sb("ol", [128, KD, S], F32R, att_mem)
        vv = sb("vv", [128, 2, D], F32, att_mem)
        n1 = sb("n1", [128, 2, 384], F32, att_mem)
        n2 = sb("n2", [128, 2, 384], F32, att_mem)
        scs = [sb(f"sc{i}", [128, 2, 384], F32, att_mem) for i in range(3)]
        pt = sb("pt", [128, 2, 384], F32, att_mem)
        two = ExitStack()
        qT = [sb(f"qT{i}", [128, 2, S], F32, two) for i in range(2)]
        kT = [sb(f"kT{i}", [128, 2, S], F32, two) for i in range(2)]
        bm = [sb(f"bm{i}", [128, 4, 384], F32, two) for i in range(2)]
        bw = [sb(f"bw{i}", [128, 4, S], F32, two) for i in range(1)]
        two.close()
        mla = ExitStack()
        qM = [sb(f"qM{i}", [96, 4, S], F32, mla) for i in range(2)]
        kM = [sb(f"kM{i}", [96, 4, S], F32, mla) for i in range(2)]
        cc = sb("cc", [128, 2, 672], F32, mla)
        kr = sb("kr", [128, 2, 32], F32, mla)
        ch, cl = oh[:, 3:8, :], ol[:, 3:8, :]
        mla.close()
        att_mem.close()

        pool_mem = ExitStack()
        zz = sb("zz", [128, 2, D], F32, pool_mem)
        pool_mem.close()

        bank = [ctx.enter_context(nc.psum_tensor(f"bank{i}", [128, 512], F32)) for i in range(4)]
        SB = ctx.enter_context(nc.psum_tensor("SB", [128, 2, 512], F32))
        TB = ctx.enter_context(nc.psum_tensor("TB", [128, 2, 512], F32))

        def cst(name):
            n = dict(CONSTS)[name]
            return con[:, CON_AT[name]:CON_AT[name] + n]

        def vcol(name, i):
            return vec[:, VEC_AT[name] + i:VEC_AT[name] + i + 1]

        ident = cst("ident")

        t_x, t_x2, t_vec, t_con = (s_x, 16), (s_x2, 16), (s_vec, 16), (s_con, 16)
        SP.quiet(lambda e: e.dma_start(vec[:, :], dram["vec"]).then_inc(s_vec, 16))
        SP.quiet(lambda e: e.dma_start(xT[:, 0:4, :], dram["x"][:, 0:4, :]).then_inc(s_x, 16))
        t_ones = DV.do(lambda e: e.memset(ones[:, :], 1.0))

        hi_t, lo_t, used = {}, {}, {}
        stream = {"dma": 0, "hi": 0, "lo": 0}

        def load_unit():
            n = stream["dma"]
            if n >= len(plan):
                return
            name, i, nk, w = plan[n]
            SP.wait(lo_t.get(n - RAW))
            SP.quiet(lambda e: e.dma_start(raw[n % RAW][:, 0:nk * w], dram[name][i]).then_inc(s_raw[n % RAW], 16))
            stream["dma"] += 1

        def raw_here(n):
            return (s_raw[n % RAW], 16 * (n // RAW + 1))

        def split_hi():
            n = stream["hi"]
            if n >= len(plan) or (n >= RING and n - RING not in used):
                return False
            _, _, nk, w = plan[n]
            hi_t[n] = AC.do(lambda e: e.activation(whi[n % RING][:, 0:nk * w], raw[n % RAW][:, 0:nk * w], ACT.Copy),
                            raw_here(n), used.get(n - RING))
            stream["hi"] += 1
            return True

        def split_lo():
            n = stream["lo"]
            if n >= stream["hi"]:
                return
            _, _, nk, w = plan[n]
            lo_t[n] = DV.do(lambda e: e.tensor_tensor(wlo[n % RING][:, 0:nk * w], raw[n % RAW][:, 0:nk * w],
                                                      whi[n % RING][:, 0:nk * w].bitcast(F32), ALU.subtract),
                            hi_t[n], raw_here(n), used.get(n - RING))
            stream["lo"] += 1
            load_unit()

        def ahead(n):
            if lazy["on"]:
                ready(n)
                lazy["n"] = n
                return
            while stream["hi"] < n + LOOK + 2 and split_hi():
                if stream["hi"] > 1:
                    split_lo()
            while stream["lo"] < min(stream["hi"], n + LOOK + 1):
                split_lo()

        lazy = {"on": False, "n": 0}

        def catch_up():
            if stream["hi"] < lazy["n"] + LOOK + 2:
                split_hi()
            if stream["lo"] < min(stream["hi"], lazy["n"] + LOOK + 1):
                split_lo()

        def ready(n):
            while stream["lo"] <= n:
                if stream["hi"] <= stream["lo"]:
                    assert split_hi()
                split_lo()

        def unit(n):
            _, _, nk, w = plan[n]
            r = n % RING
            return (whi[r][:, 0:nk * w].rearrange("p (k n) -> p k n", k=nk),
                    wlo[r][:, 0:nk * w].rearrange("p (k n) -> p k n", k=nk))

        at = {"unit": 0}

        def next_unit():
            at["unit"] += 1
            return at["unit"] - 1

        free = [[] for _ in range(4)]
        turn = {"n": 0}
        held = set()

        def take():
            while True:
                b = turn["n"] % 4
                turn["n"] += 1
                if b not in held:
                    return b

        def hold():
            b = take()
            held.add(b)
            return b

        def three(po, ah, al, bh, bl, start, stop, tokens=(), done=False):
            PE.quiet(lambda e: e.matmul(po, ah, bh, start=start, stop=False, skip_group_check=True), *tokens)
            PE.quiet(lambda e: e.matmul(po, ah, bl, start=False, stop=False, skip_group_check=True))
            last = lambda e: e.matmul(po, al, bh, start=False, stop=stop, skip_group_check=True)
            if done:
                return PE.do(last)
            PE.quiet(last)

        def tensorT(n, b, k0, k1, ch_t, act_h, act_l, first, last, kk=0, mt=2):
            wh, wl = unit(n)
            po = bank[b][:, :].rearrange("p (m s) -> p m s", m=2)
            tok = None
            for k in range(k0, k1):
                for m in range(mt):
                    end = last and k == k1 - 1
                    waits = [hi_t[n], lo_t[n], *ch_t(k + kk)] + (free[b] if first and k == k0 and m == 0 else [])
                    tok = three(po[:, m, :], wh[:, k, m * 128:(m + 1) * 128], wl[:, k, m * 128:(m + 1) * 128],
                                act_h[:, k + kk, :], act_l[:, k + kk, :],
                                start=(first and k == k0 and m == 0), stop=end,
                                tokens=waits, done=(k == k1 - 1 and m == mt - 1))
            return tok

        x_t = [None] * KD
        xs_t = [[None, None] for _ in range(KD)]

        def split_x_hi(k, gain, gi):
            g = vcol(gain, gi) if isinstance(gain, str) else gain[:, gi:gi + 1]
            a = AC.do(lambda e: e.activation(xh[:, k, :], xT[:, k, :], ACT.Copy, scale=g), x_t[k], t_vec, PE.now())

            def low():
                d = DV.do(lambda e: e.scalar_tensor_tensor(out=xl[:, k, :], in0=xT[:, k, :], scalar=g,
                                                           in1=xh[:, k, :].bitcast(F32), op0=ALU.mult,
                                                           op1=ALU.subtract), a)
                xs_t[k] = [a, d]
            return low

        def split_x(k, gain, gi):
            split_x_hi(k, gain, gi)()

        ss_t, ss2 = {"t": None}, {"t": None, "sq": None}
        sq_free = {"t": None}

        def squares(c, later=False):
            if c == 0:
                ss_t["t"] = AC.do(lambda e: e.activation(ssum[:, :, :], xT[:, 0:2, :], ACT.Square),
                                  x_t[0], x_t[1], PE.now())
                return lambda: None
            dst = sq2 if later and c == 2 else sq
            a = AC.do(lambda e: e.activation(dst[:, :, :], xT[:, 2 * c:2 * c + 2, :], ACT.Square),
                      x_t[2 * c], x_t[2 * c + 1], sq_free["t"], ss2["t"])

            def add():
                ss_t["t"] = sq_free["t"] = DV.do(
                    lambda e: e.tensor_tensor(ssum[:, :, :], ssum[:, :, :], dst[:, :, :], ALU.add), a, ss_t["t"])
            if later:
                return add
            add()

        def scaled_squares(c):
            dst = ssum2 if c == 0 else sq2
            for m in range(2):
                a = AC.do(lambda e, m=m: e.activation(dst[:, m, :], xT[:, 2 * c + m, :], ACT.Square,
                                                      scale=vcol("norm_final", 2 * c + m)), x_t[2 * c + m],
                          ss2["sq"], t_vec)
            ss2["t"] = a if c == 0 else DV.do(lambda e: e.tensor_tensor(ssum2[:, :, :], ssum2[:, :, :], sq2[:, :, :],
                                                                        ALU.add), a, ss2["t"])
            ss2["sq"] = ss2["t"] if c else None

        def rsqrt(v, y, t, tok):
            tok = DV.do(lambda e: e.tensor_scalar(t.bitcast(I32), v.bitcast(I32), 1, None,
                                                  ALU.logical_shift_right), tok)
            tok = DV.do(lambda e: e.tensor_scalar(y.bitcast(I32), t.bitcast(I32), -1.0, MAGIC, ALU.mult,
                                                  ALU.add), tok)
            for _ in range(3):
                tok = DV.do(lambda e: e.scalar_tensor_tensor(out=t, in0=y, scalar=-0.5, in1=v, op0=ALU.mult,
                                                             op1=ALU.mult), tok)
                tok = DV.do(lambda e: e.tensor_tensor(t, t, y, ALU.mult), tok)
                tok = DV.do(lambda e: e.scalar_tensor_tensor(out=y, in0=t, scalar=1.5, in1=y, op0=ALU.add,
                                                             op1=ALU.mult), tok)
            return tok

        s_free, tb_free = {"t": []}, {"t": []}
        rcol, rv, rt = small[:, 0, 0:2], small[:, 1, 0:2], small[:, 2, 0:2]
        r_t, dg_free = {"col": None, "row": None}, {"t": None}

        def token_sums(src, dst, tok):
            for h in range(2):
                for c in range(2):
                    fn = lambda e, h=h, c=c: e.matmul(dst[:, h:h + 1], src[:, c, h * 128:(h + 1) * 128],
                                                      ones[:, 0:1], start=(h == 0 and c == 0), stop=(c == 1),
                                                      skip_group_check=True)
                    if h == 1 and c == 1:
                        return PE.do(fn)
                    PE.quiet(fn, tok, t_ones, *s_free["t"])

        def rms_col():
            m = token_sums(ssum, SB[:, 0, :], ss_t["t"])
            v = DV.do(lambda e: e.tensor_scalar(rv, SB[:, 0, 0:2], 1.0 / D, EPS, ALU.mult, ALU.add), m, AC.now(),
                      PE.now())
            s_free["t"] = [v]
            r_t["col"] = rsqrt(rv, rcol, rt, v)

        def rms_row(col=None, row=None, q=0):
            col = rcol if col is None else col
            row = rb if row is None else row
            for h in range(2):
                t = DV.do(lambda e, h=h: e.tensor_scalar(dg[:, h, :], ident, col[:, h:h + 1], None, ALU.mult),
                          r_t["col"], t_con, dg_free["t"])
            PE.quiet(lambda e: e.matmul(TB[:, q, 0:128], ones[:, :], dg[:, 0, :], start=True, stop=True,
                                        skip_group_check=True), t, *tb_free["t"])
            m = PE.do(lambda e: e.matmul(TB[:, q, 128:256], ones[:, :], dg[:, 1, :], start=True, stop=True,
                                         skip_group_check=True))
            dg_free["t"] = m
            r_t["row"] = DV.do(lambda e: e.tensor_copy(row[:, :], TB[:, q, 0:256]), m)
            tb_free["t"] = [r_t["row"]]

        def residual(b, c, tok, gain=None, gi=0, sums=True):
            r = DV.do(lambda e: e.tensor_tensor(xT[:, 2 * c:2 * c + 2, :].rearrange("p k s -> p (k s)"),
                                                bank[b][:, :], xT[:, 2 * c:2 * c + 2, :].rearrange("p k s -> p (k s)"),
                                                ALU.add), tok, *xs_t[2 * c], *xs_t[2 * c + 1], AC.now())
            free[b] = [r]
            x_t[2 * c] = x_t[2 * c + 1] = r
            if sums:
                squares(c)
            if sums == 2:
                scaled_squares(c)
            if gain is not None:
                for k in (2 * c, 2 * c + 1):
                    split_x(k, gain, gi + k)

        def ffn(layer, func, next_gain, next_gi, sums=True):
            cw = lambda tap, f: vcol("conv_w", (layer * 3 + tap) * NF + f)
            cb = lambda f: vcol("conv_b", layer * NF + f)
            late = []
            xw = lambda k: xs_t[k]
            for i in range(2):
                pads = DV.do(lambda e, i=i: e.memset(gp[i][:, :, 0:2], 0.0), PE.now(), AC.now())

            conv = [None, None]
            hs_t = [[None, None] for _ in range(NF)]

            def evacuate(i, bg, bu, tg, tu, top):
                g, ct, ub = gp[i % 2], cts[i % 2], ubs[i % 2]
                rbb = rb[:, :].unsqueeze(1).to_broadcast([128, 2, S])
                pg = bank[bg][:, :].rearrange("p (m s) -> p m s", m=2)
                pu = bank[bu][:, :].rearrange("p (m s) -> p m s", m=2)
                d0 = DV.do(lambda e: e.tensor_tensor(g[:, :, 2:S + 2], pg, rbb, ALU.mult), tg, r_t["row"], pads,
                           conv_read.get(i - 2))
                free[bg] = [d0]
                rest = late.pop(0)() if late else None
                a0 = AC.do(lambda e: e.activation(ct[:, 0, :], g[:, 0, 0:S], ACT.Identity, scale=cw(0, 2 * i),
                                                  bias=cb(2 * i)), d0)
                a1 = AC.do(lambda e: e.activation(ct[:, 1, :], g[:, 1, 0:S], ACT.Identity, scale=cw(0, 2 * i + 1),
                                                  bias=cb(2 * i + 1)), d0)
                if rest:
                    rest[0]()
                if stream["hi"] <= top:
                    split_hi()
                if stream["lo"] < stream["hi"] - 1:
                    split_lo()
                if rest:
                    rest[1]()
                d1 = DV.do(lambda e: e.tensor_tensor(ub[:, :, :], pu, rbb, ALU.mult), tu)
                free[bu] = [d1]
                for tap in (1, 2):
                    for m, a in ((0, a0), (1, a1)):
                        conv[m] = DV.do(lambda e, tap=tap, m=m: e.scalar_tensor_tensor(
                            out=ct[:, m, :], in0=g[:, m, tap:S + tap], scalar=cw(tap, 2 * i + m), in1=ct[:, m, :],
                            op0=ALU.mult, op1=ALU.add), a, conv[m])
                conv_read[i] = conv[1]
                if stream["hi"] <= top:
                    split_hi()
                if stream["lo"] < stream["hi"] - 1:
                    split_lo()
                a2 = AC.do(lambda e: e.activation(ct[:, :, :], ct[:, :, :], func), *conv)
                while stream["hi"] <= top and split_hi():
                    if stream["lo"] < stream["hi"] - 1:
                        split_lo()

                def finish():
                    d3 = DV.do(lambda e: e.tensor_tensor(hb[:, :, :], ct[:, :, :], ub[:, :, :], ALU.mult), a2, d1,
                               hs_t[2 * i - 1][0])
                    tk = {}

                    def high():
                        tk["a"] = AC.do(lambda e: e.activation(hh[:, 2 * i:2 * i + 2, :], hb[:, :, :], ACT.Copy), d3)

                    def low():
                        d4 = DV.do(lambda e: e.tensor_tensor(hl[:, 2 * i:2 * i + 2, :], hb[:, :, :],
                                                             hh[:, 2 * i:2 * i + 2, :].bitcast(F32), ALU.subtract),
                                   tk["a"])
                        hs_t[2 * i] = hs_t[2 * i + 1] = [tk["a"], d4]
                    return high, low
                late.append(finish)

            conv_read = {}
            for i in range(11):
                n0, n1_ = next_unit(), next_unit()
                ready(n1_)
                bg, bu = take(), take()
                if i == 0:
                    ready(n1_ + 2)
                    for k in range(KD):
                        tg = tensorT(n0, bg, k, k + 1, xw, xh, xl, k == 0, k == KD - 1)
                        tu = tensorT(n1_, bu, k, k + 1, xw, xh, xl, k == 0, k == KD - 1)
                        if k == KD - 1:
                            rms_col()
                    used[n0] = used[n1_] = tu
                    first = (i, bg, bu, tg, tu, n0 + 6)
                    continue
                else:
                    if i == 1:
                        tensorT(n0, bg, 0, 5, xw, xh, xl, True, False)
                        rms_row()
                        tg = used[n0] = tensorT(n0, bg, 5, KD, xw, xh, xl, False, True)
                        evacuate(*first)
                    else:
                        tg = used[n0] = tensorT(n0, bg, 0, KD, xw, xh, xl, True, True)
                    tu = used[n1_] = tensorT(n1_, bu, 0, KD, xw, xh, xl, True, True)
                evacuate(i, bg, bu, tg, tu, n0 + 6)
            for fn in late.pop(0)():
                fn()
            for c in range(4):
                b = take()
                k0 = 0
                for j, nk in enumerate((8, 8, 6)):
                    n = next_unit()
                    ahead(n)
                    t = used[n] = tensorT(n, b, 0, nk, lambda k: hs_t[k], hh, hl, j == 0, j == 2, kk=k0)
                    if c == 3 and j == 2 and layer < 3:
                        ready(n + 3)
                    k0 += nk
                residual(b, c, t, next_gain, next_gi, sums)

        def natural(n, banks, act_h, act_l, act_t, halves=None):
            wh, wl = unit(n)
            _, _, nk, w = plan[n]
            toks = []
            for h in (range(2) if halves is None else halves):
                b = banks[h % len(banks)]
                po = bank[b][:, 0:w] if len(banks) == 2 else bank[b][:, h * 256:h * 256 + w]
                new = len(banks) == 2 or h == 0
                for k in range(nk):
                    waits = [hi_t[n], lo_t[n], *act_t(k)] + (free[b] if k == 0 and new else [])
                    sl = slice(h * 128, (h + 1) * 128)
                    tok = three(po, act_h[:, k, sl], act_l[:, k, sl], wh[:, k, :], wl[:, k, :],
                                start=(k == 0), stop=(k == nk - 1), tokens=waits, done=(k == nk - 1))
                toks.append(tok)
            return toks

        def stat(i, j):
            return small[:, 3 + i, 4 * (j % 3):4 * (j % 3) + 4]

        sc_free = [[], [], []]
        pt_t, o_t = {}, {}
        pt_free = {"t": []}
        p_t = {}
        v_t = {}

        def scores(j, heads, scale, mask, m_t):
            sc, mxs, nms, lsum = scs[j % 3], stat(0, j), stat(1, j), stat(2, j)
            for a, (q, k, toks) in enumerate(heads):
                PE.quiet(lambda e, a=a, q=q, k=k: e.matmul(SB[:, a, 0:128], q[:, 0:128], k[:, 0:128], start=True,
                                                           stop=True, skip_group_check=True), *toks, *s_free["t"])
                m = PE.do(lambda e, a=a, q=q, k=k: e.matmul(SB[:, a, 128:384], q[:, 128:256], k[:, 0:256],
                                                            start=True, stop=True, skip_group_check=True))
            d = DV.do(lambda e: e.scalar_tensor_tensor(out=sc[:, :, :], in0=SB[:, :, 0:384], scalar=scale, in1=mask,
                                                       op0=ALU.mult, op1=ALU.add), m, *m_t, *sc_free[j % 3])
            s_free["t"] = [d]
            d1 = DV.do(lambda e: e.tensor_reduce(mxs[:, 0:2], sc[:, :, 0:128], AX_X, ALU.max), d)
            d2 = DV.do(lambda e: e.tensor_reduce(mxs[:, 2:4], sc[:, :, 128:384], AX_X, ALU.max), d)
            d3 = DV.do(lambda e: e.tensor_scalar(nms, mxs, -1.0, None, ALU.mult), d1, d2)
            for a in range(2):
                for h, sl in ((0, slice(0, 128)), (1, slice(128, 384))):
                    x = AC.do(lambda e, a=a, h=h, sl=sl: e.activation(
                        sc[:, a, sl], sc[:, a, sl], ACT.Exp, bias=nms[:, 2 * h + a:2 * h + a + 1],
                        accum_out=lsum[:, 2 * h + a:2 * h + a + 1]), d3)
            p_t[j] = x

        def normalize(j):
            sc, lsum, linv = scs[j % 3], stat(2, j), stat(3, j)
            d = DV.do(lambda e: e.reciprocal(linv, lsum), p_t[j])
            for a in range(2):
                for h, sl in ((0, slice(0, 128)), (1, slice(128, 384))):
                    x = DV.do(lambda e, a=a, h=h, sl=sl: e.tensor_scalar(
                        sc[:, a, sl], sc[:, a, sl], linv[:, 2 * h + a:2 * h + a + 1], None, ALU.mult), d)
            p_t[j] = x

        def transposes(j):
            sc = scs[j % 3]
            for a in range(2):
                for c in range(3):
                    m = PE.do(lambda e, a=a, c=c: e.transpose(TB[:, a, c * 128:(c + 1) * 128],
                                                              sc[:, a, c * 128:(c + 1) * 128], ident),
                              p_t[j], *tb_free["t"])
            sc_free[j % 3] = [m]
            x = AC.do(lambda e: e.activation(pt[:, :, :], TB[:, :, 0:384], ACT.Copy), m, *pt_free["t"])
            tb_free["t"] = [x]
            pt_t[j] = x

        def values(j):
            b = take()
            for a in range(2):
                o = slice(64 * a, 64 * a + 64)
                col = slice((2 * j + a) * 64, (2 * j + a) * 64 + 64)
                PE.quiet(lambda e, a=a, o=o, col=col: e.matmul(bank[b][o, 0:128], vv[:, 0, col], pt[:, a, 0:128],
                                                               start=True, stop=True, skip_group_check=True),
                         pt_t[j], *v_t[j // 2], *free[b])
                PE.quiet(lambda e, a=a, o=o, col=col: e.matmul(bank[b][o, 128:256], vv[:, 0, col], pt[:, a, 128:256],
                                                               start=True, stop=False, skip_group_check=True))
                m = PE.do(lambda e, a=a, o=o, col=col: e.matmul(bank[b][o, 128:256], vv[:, 1, col],
                                                                pt[:, a, 256:384], start=False, stop=True,
                                                                skip_group_check=True))
            pt_free["t"] = [m]
            a_ = AC.do(lambda e: e.activation(oh[:, j, :], bank[b][:, 0:256], ACT.Copy), m)
            d_ = DV.do(lambda e: e.tensor_tensor(ol[:, j, :], bank[b][:, 0:256], oh[:, j, :].bitcast(F32),
                                                 ALU.subtract), a_)
            free[b] = [a_, d_]
            o_t[j] = [a_, d_]

        def project_out(gain, gi, sums=True):
            n0, n1_ = next_unit(), next_unit()
            bb = [None, None]
            st = {}
            ow = lambda k: o_t[k]

            def piece(ks):
                def run():
                    for k in ks:
                        if k == 0:
                            ahead(n0)
                            ahead(n1_)
                            st["b"] = (hold(), hold())
                        b0, b1 = st["b"]
                        st["t0"] = tensorT(n0, b0, k, k + 1, ow, oh, ol, k == 0, k == KD - 1)
                        st["t1"] = tensorT(n1_, b1, k, k + 1, ow, oh, ol, k == 0, k == KD - 1)
                return run

            def finish():
                used[n0] = used[n1_] = st["t1"]
                held.clear()
                ready(n0 + 5)
                for c in (2, 3):
                    n = next_unit()
                    b = take()
                    t = used[n] = tensorT(n, b, 0, KD, ow, oh, ol, True, True)
                    if c == 2:
                        residual(st["b"][0], 0, st["t1"], gain, gi, sums)
                        residual(st["b"][1], 1, st["t1"], gain, gi, sums)
                    residual(b, c, t, gain, gi, sums)

            return (lambda ks: piece(ks)()), finish

        def heads_mixer(kind, gain, gi):
            last = {}
            rc = {}

            def begin():
                rms_col()
                if kind == 0:
                    for h in range(2):
                        for nm, c in (("cos0", 0), ("sin0", 1)):
                            rc["t"] = DV.do(lambda e, h=h, nm=nm, c=c: e.tensor_scalar(
                                crs[:, c, h, :], cst(nm)[:, h * 64:(h + 1) * 64], rcol[:, h:h + 1], None, ALU.mult),
                                r_t["col"], t_con)

            def group(g):
                ns, st = {}, {}

                def half(part, h):
                    def run():
                        if h == 0:
                            ns[part] = next_unit()
                        n = ns[part]
                        if h == 0:
                            ahead(n)
                            st[part] = hold()
                        st[part, h] = natural(n, [st[part]], xh, xl, lambda k: xs_t[k], halves=[h])[0]
                        if h == 1:
                            used[n] = st[part, 1]
                            held.discard(st[part])
                            if g == 0 and part == 1:
                                begin()
                            evacuate(part)
                    return run

                def evacuate(part):
                    b, t = st[part], st[part, 1]
                    if part == 2:
                        for h in range(2):
                            a = AC.do(lambda e, h=h: e.activation(vv[:, h, g * 256:(g + 1) * 256],
                                                                  bank[b][:, h * 256:(h + 1) * 256], ACT.Copy,
                                                                  scale=rcol[:, h:h + 1]), t, r_t["col"])
                        free[b] = [a]
                        v_t[g] = [a]
                        return
                    dst = n1 if part == 0 else n2
                    flat = dst[:, :, 0:256]
                    if kind == 0:
                        tmp = rtmp
                        ps = bank[b][:, :].rearrange("p (t h d) -> p t h d", t=2, h=4)
                        fl = flat.rearrange("p t (h d) -> p t h d", h=4)
                        tm = tmp[:, :, 0:256].rearrange("p t (h d) -> p t h d", h=4)
                        wide = lambda c, lo, n: crs[:, c, :, lo:lo + n].unsqueeze(2).to_broadcast([128, 2, 4, n])
                        for q in range(2):
                            src = slice(32 - 32 * q, 64 - 32 * q)
                            d1 = DV.do(lambda e, q=q, src=src: e.tensor_tensor(
                                tm[:, :, :, 32 * q:32 * q + 32], ps[:, :, :, src], wide(1, 32 * q, 32), ALU.mult),
                                t, rc["t"], last.get("tmp"))
                        for h in range(2):
                            d0 = DV.do(lambda e, h=h: e.tensor_tensor(
                                fl[:, h], ps[:, h], crs[:, 0, h, :].unsqueeze(1).to_broadcast([128, 4, 64]),
                                ALU.mult), t, rc["t"], last.get(part))
                        free[b] = [d0, d1]
                        d = DV.do(lambda e: e.tensor_tensor(flat, flat, tmp[:, :, 0:256], ALU.add), d0, d1)
                        last["tmp"] = d
                        st["n", part] = d
                    else:
                        for h in range(2):
                            a = AC.do(lambda e, h=h: e.activation(flat[:, h, :], bank[b][:, h * 256:(h + 1) * 256],
                                                                  ACT.Copy, scale=rcol[:, h:h + 1]),
                                      t, r_t["col"], last.get(part))
                        free[b] = [a]
                        x = AC.do(lambda e: e.activation(rtmp[:, :, 0:256], flat, ACT.Square), a, last.get("tmp"))
                        ss = small[:, 7, 0:8]
                        vs = small[:, 8, 0:8]
                        ys = small[:, 9 + part, 0:8]
                        tt = small[:, 11, 0:8]
                        d = DV.do(lambda e: e.tensor_reduce(
                            ss.rearrange("p (t h) -> p t h", t=2),
                            rtmp[:, :, 0:256].rearrange("p t (h d) -> p t h d", h=4), AX_X, ALU.add), x)
                        last["tmp"] = d
                        d = DV.do(lambda e: e.tensor_scalar(vs, ss, 1.0 / 64, EPS, ALU.mult, ALU.add), d)
                        d = rsqrt(vs, ys, tt, d)
                        for h in range(2):
                            f4 = flat[:, h, :].rearrange("p (h d) -> p h d", h=4)
                            st["n", part] = DV.do(lambda e, h=h, f4=f4: e.tensor_tensor(
                                f4, f4, ys[:, 4 * h:4 * h + 4].unsqueeze(2).to_broadcast([128, 4, 64]), ALU.mult), d)

                def turn_over(part):
                    def run():
                        src = n1 if part == 0 else n2
                        dst = (qT if part == 0 else kT)[g % 2]
                        b = take()
                        for c in range(2):
                            for h in range(2):
                                m = PE.do(lambda e, c=c, h=h: e.transpose(
                                    bank[b][:, c * 256 + h * 128:c * 256 + (h + 1) * 128],
                                    src[:, h, c * 128:(c + 1) * 128], ident), st["n", part], t_con, *free[b])
                        last[part] = m
                        kw = {"scale": vcol("q_norm" if part == 0 else "k_norm", 0)} if kind == 3 else {}
                        a = AC.do(lambda e: e.activation(dst[:, :, :].rearrange("p c s -> p (c s)"), bank[b][:, :],
                                                         ACT.Copy, **kw), m, PE.now())
                        free[b] = [a]
                        tt_t[g, part] = a
                    return run

                def bias():
                    if kind == 3:
                        load = (s_bias[0], 16 * (g + 1))
                        SP.wait(bw_free["t"], bm_t.get(g - 1))
                        SP.quiet(lambda e: e.dma_start(bw[0][:, :, :], dram["bias"][g]).then_inc(s_bias[0], 16))
                        m3 = cst("mask3")
                        p0 = PO.do(lambda e: e.tensor_tensor(
                            bm[g % 2][:, :, 0:128], bw[0][:, :, 128:256],
                            m3[:, 0:128].unsqueeze(1).to_broadcast([128, 4, 128]), ALU.add),
                            load, t_con, sc_read[g - 2] if g >= 2 else None)
                        p1 = PO.do(lambda e: e.tensor_tensor(
                            bm[g % 2][:, :, 128:384], bw[0][:, :, :],
                            m3[:, 128:384].unsqueeze(1).to_broadcast([128, 4, 256]), ALU.add))
                        bm_t[g] = p1
                return half, turn_over, bias

            tt_t, bm_t, sc_read = {}, {}, {}
            bw_free = {"t": PE.now()}

            def pair_heads(j):
                g, c = j // 2, j % 2
                tk = [tt_t[g, 0], tt_t[g, 1]]
                return [(qT[g % 2][64 * a:64 * a + 64, c, :], kT[g % 2][64 * a:64 * a + 64, c, :], tk)
                        for a in range(2)]

            def mask_of(j):
                if kind == 0:
                    return cst("mask0").unsqueeze(1).to_broadcast([128, 2, 384]), [t_con]
                g, c = j // 2, j % 2
                return bm[g % 2][:, 2 * c:2 * c + 2, :], [bm_t[g]]

            groups = [group(g) for g in range(NG)]
            half, turn_over, bias = groups[0]
            bias()
            for p in (half(1, 0), half(1, 1), half(0, 0), half(0, 1), half(2, 0), turn_over(1), half(2, 1),
                      groups[1][0](1, 0)):
                p()

            def slots_of(g):
                turn_q = groups[g][1](0)
                if g == 3:
                    return [[turn_q], [groups[3][0](2, 1)], [], []]
                half, turn_over, bias = groups[g + 1]
                bias()
                after = groups[g + 2][0](1, 0) if g < 2 else half(2, 0)
                v = [half(2, 0)], [turn_over(1), half(2, 1)]
                if g == 2:
                    v = [], [turn_over(1)]
                return [[half(1, 1), turn_q], [half(0, 0)], [], [], [half(0, 1)], *v, [after]]

            sc_free[0] = sc_free[1] = sc_free[2] = [PE.now()]
            weave(slots_of, pair_heads, 0.125, mask_of, gain, gi, sc_read)

        def weave(slots_of, pair_heads, scale, mask_of, gain, gi, sc_read):
            def run(pieces):
                for p in pieces:
                    p()

            def step(j, slots):
                if j >= 1:
                    normalize(j - 1)
                run(slots[0])
                if j >= 2:
                    transposes(j - 2)
                scores(j, pair_heads(j), scale, *mask_of(j))
                catch_up()
                run(slots[1])
                if j >= 2:
                    values(j - 2)
                catch_up()
                run(slots[2])
                run(slots[3])

            lazy["on"], lazy["n"] = True, at["unit"] - 1
            for g in range(3):
                slots = slots_of(g)
                step(2 * g, slots[0:4])
                step(2 * g + 1, slots[4:])
                sc_read[g] = DV.now()
            slots = slots_of(3)
            step(6, slots)
            wo, finish = project_out(gain, gi)
            step(7, [[], [lambda: wo([0, 1])], [lambda: wo([2, 3])], [lambda: wo([4])]])
            normalize(7)
            transposes(6)
            wo([5])
            values(6)
            transposes(7)
            catch_up()
            wo([6])
            values(7)
            wo([7])
            lazy["on"] = False
            finish()

        def latent_mixer(gain, gi):
            tcol = small[:, 12, 0:4]
            c_t = {}
            banks_of = {}
            ns = [next_unit() for _ in range(3)]
            ahead(ns[0])
            for i, n in enumerate(ns):
                ahead(n)
                w = plan[n][3]
                b = take()
                t = used[n] = natural(n, [b], xh, xl, lambda k: xs_t[k])[-1]
                if i == 0:
                    rms_col()
                for h in range(2):
                    a = AC.do(lambda e, h=h, b=b, i=i, w=w: e.activation(
                        cc[:, h, i * 256:i * 256 + w], bank[b][:, h * 256:h * 256 + w], ACT.Copy,
                        scale=rcol[:, h:h + 1]), t, r_t["col"])
                free[b] = [a]
                c_t[i] = a
                if i:
                    latent_chunks(c_t[i - 1], (0, 1) if i == 1 else (2, 3))
            latent_chunks(c_t[2], (4,))
            lv, ly, lt = small[:, 13, 0:4], small[:, 14, 0:4], small[:, 15, 0:4]
            for h in range(2):
                AC.do(lambda e, h=h: e.activation(n1[:, 0, 0:384], cc[:, h, 0:384], ACT.Square,
                                                  accum_out=tcol[:, h:h + 1]), c_t[2], AC.now())
                a = AC.do(lambda e, h=h: e.activation(n1[:, 1, 0:256], cc[:, h, 384:640], ACT.Square,
                                                      accum_out=tcol[:, 2 + h:3 + h]), AC.now())
            d = DV.do(lambda e: e.tensor_scalar(lv[:, 0:2], tcol[:, 0:2], 1.0 / 384, EPS, ALU.mult, ALU.add), a)
            d = DV.do(lambda e: e.tensor_scalar(lv[:, 2:4], tcol[:, 2:4], 1.0 / 256, EPS, ALU.mult, ALU.add), a)
            l_t = rsqrt(lv, ly, lt, d)
            cs, sn = (cst(x).rearrange("p (t d) -> p t d", t=2) for x in ("cos1", "sin1"))
            krs = cc[:, :, 640:672]
            d = DV.do(lambda e: e.tensor_tensor(kr[:, :, :], krs, cs, ALU.mult), c_t[2], t_con)
            tmp = rtmp[:, :, 0:32]
            d1 = DV.do(lambda e: e.tensor_tensor(tmp[:, :, 0:16], krs[:, :, 16:32], sn[:, :, 0:16], ALU.mult))
            d1 = DV.do(lambda e: e.tensor_tensor(tmp[:, :, 16:32], krs[:, :, 0:16], sn[:, :, 16:32], ALU.mult))
            kr_t = DV.do(lambda e: e.tensor_tensor(kr[:, :, :], kr[:, :, :], tmp, ALU.add), d, d1)
            last = {}
            tt_t = {}

            def group(g):
                st = {}

                def q_half(h):
                    def run():
                        if h == 0:
                            st["nq"] = next_unit()
                            ahead(st["nq"])
                        b = take()
                        nq = st["nq"]
                        t = natural(nq, [b, b], ch, cl, lambda k: cs_t[k], halves=[h])[0]
                        if h == 1:
                            used[nq] = t
                        a = AC.do(lambda e: e.activation(n1[:, h, :], bank[b][:, 0:384], ACT.Copy,
                                                         scale=ly[:, h:h + 1]), t, l_t, last.get("q"))
                        free[b] = [a]
                        if h == 1:
                            nr = n1[:, :, :].rearrange("p t (h d) -> p t h d", h=4)[:, :, :, 64:96]
                            tm = rtmp[:, :, 0:128].rearrange("p t (h d) -> p t h d", h=4)
                            wide = lambda x, lo, n: x[:, :, lo:lo + n].unsqueeze(2).to_broadcast([128, 2, 4, n])
                            d1 = DV.do(lambda e: e.tensor_tensor(tm[:, :, :, 0:16], nr[:, :, :, 16:32],
                                                                 wide(sn, 0, 16), ALU.mult), a, DV.now())
                            d1 = DV.do(lambda e: e.tensor_tensor(tm[:, :, :, 16:32], nr[:, :, :, 0:16],
                                                                 wide(sn, 16, 16), ALU.mult))
                            for tt in range(2):
                                d0 = DV.do(lambda e, tt=tt: e.tensor_tensor(
                                    nr[:, tt], nr[:, tt], cs[:, tt, :].unsqueeze(1).to_broadcast([128, 4, 32]),
                                    ALU.mult), d1)
                            for tt in range(2):
                                d = DV.do(lambda e, tt=tt: e.tensor_tensor(nr[:, tt], nr[:, tt], tm[:, tt],
                                                                           ALU.add), d0, d1)
                            st["q"] = d
                    return run

                def kv_half(h):
                    def run():
                        if h == 0:
                            st["nkv"] = next_unit()
                            ahead(st["nkv"])
                        b = take()
                        nkv = st["nkv"]
                        t = natural(nkv, [b, b], ch[:, 3:5, :], cl[:, 3:5, :], lambda k: cs_t[3 + k], halves=[h])[0]
                        if h == 1:
                            used[nkv] = t
                        pv = bank[b][:, :].rearrange("p (h d) -> p h d", h=4)
                        k4 = n2[:, h, :].rearrange("p (h d) -> p h d", h=4)
                        d = AC.do(lambda e: e.activation(k4[:, :, 0:64], pv[:, :, 0:64], ACT.Copy,
                                                         scale=ly[:, 2 + h:3 + h]), t, l_t, last.get("k"))
                        a = AC.do(lambda e: e.activation(
                            vv[:, h, g * 256:(g + 1) * 256].rearrange("p (h d) -> p h d", h=4), pv[:, :, 64:128],
                            ACT.Copy, scale=ly[:, 2 + h:3 + h]), t, l_t)
                        free[b] = [a]
                        p = PO.do(lambda e: e.tensor_copy(k4[:, :, 64:96],
                                                          kr[:, h, :].unsqueeze(1).to_broadcast([128, 4, 32])),
                                  kr_t, last.get("k"))
                        st["k", h] = [d, p]
                        v_t[g] = [a]
                    return run

                def turn_over(part, c):
                    def run():
                        src = n1 if part == 0 else n2
                        dst = (qM if part == 0 else kM)[g % 2]
                        b = take()
                        toks = [st["q"]] if part == 0 else st["k", 0] + st["k", 1]
                        for a_ in range(2):
                            for h in range(2):
                                hd = 2 * c + a_
                                m = PE.do(lambda e, a_=a_, h=h, hd=hd: e.transpose(
                                    bank[b][0:96, a_ * 256 + h * 128:a_ * 256 + (h + 1) * 128],
                                    src[:, h, hd * 96:(hd + 1) * 96], ident), *toks, t_con, *free[b])
                        last["q" if part == 0 else "k"] = m
                        flat = dst[:, 2 * c:2 * c + 2, :].rearrange("p c s -> p (c s)")
                        if part == 0:
                            a = AC.do(lambda e: e.activation(flat, bank[b][0:96, :], ACT.Copy), m, PE.now())
                        else:
                            a = DV.do(lambda e: e.tensor_copy(flat, bank[b][0:96, :]), m, PE.now())
                        free[b] = [a]
                        tt_t[g, part, c] = a
                    return run
                return q_half, kv_half, turn_over

            def pair_heads(j):
                g, c = j // 2, j % 2
                tk = [tt_t[g, 0, c], tt_t[g, 1, c]]
                return [(qM[g % 2][:, 2 * c + a, :], kM[g % 2][:, 2 * c + a, :], tk) for a in range(2)]

            mask_of = lambda j: (cst("mask0").unsqueeze(1).to_broadcast([128, 2, 384]), [t_con])
            groups = [group(g) for g in range(NG)]
            q, kv, turn = groups[0]
            for p in (q(0), q(1), kv(0), kv(1), turn(0, 0), turn(1, 0), turn(0, 1), turn(1, 1), groups[1][0](0)):
                p()

            def slots_of(g):
                if g == 3:
                    return [[], [], [], []]
                q, kv, turn = groups[g + 1]
                after = [groups[g + 2][0](0)] if g < 2 else []
                return [[q(1)], [kv(0)], [], [],
                        [kv(1)], [turn(0, 0), turn(0, 1)], [turn(1, 0)], [turn(1, 1), *after]]

            weave(slots_of, pair_heads, 96 ** -0.5, mask_of, gain, gi, {})

        cs_t = {}

        def latent_chunks(tok, chunks):
            for c in chunks:
                b = take()
                for h in range(2):
                    m = PE.do(lambda e, h=h, c=c, b=b: e.transpose(bank[b][:, h * 128:(h + 1) * 128],
                                                                   cc[:, h, c * 128:(c + 1) * 128], ident),
                              tok, t_con, *free[b])
                g = vcol("b_q_norm", c) if c < 3 else vcol("b_kv_norm", c - 3)
                a = AC.do(lambda e, c=c, b=b, g=g: e.activation(ch[:, c, :], bank[b][:, 0:256], ACT.Copy, scale=g), m)
                d = DV.do(lambda e, c=c, b=b, g=g: e.scalar_tensor_tensor(
                    out=cl[:, c, :], in0=bank[b][:, 0:256], scalar=g, in1=ch[:, c, :].bitcast(F32), op0=ALU.mult,
                    op1=ALU.subtract), a)
                free[b] = [a, d]
                cs_t[c] = [a, d]

        gg, bs = small[:, 7, 0:8], small[:, 8, 0:8]

        def pool_gains():
            v = lambda name: vec[:, VEC_AT[name]:VEC_AT[name] + 8]
            DV.do(lambda e: e.tensor_tensor(gg, v("norm_final"), v("mix_norm_2"), ALU.mult), t_vec)
            t = DV.do(lambda e: e.tensor_tensor(bs, v("pool_b"), v("pool_scale"), ALU.mult))
            AC.wait(t)
            SP.wait(PE.now(), AC.now(), DV.now(), PO.now())
            SP.quiet(lambda e: e.dma_start(wins[:, :, :], dram["win"]).then_inc(s_win, 16))

        def pool_mixer(next_gain, next_gi):
            n = next_unit()
            wh, wl = unit(n)
            done_t = {}

            def product(g):
                b = take()
                for k in (2 * g, 2 * g + 1):
                    for h in range(2):
                        sl = slice(h * 128, (h + 1) * 128)
                        t = three(bank[b][:, h * 256:(h + 1) * 256], xh[:, k, sl], xl[:, k, sl], wh[:, k, :],
                                  wl[:, k, :], start=(k == 2 * g and h == 0), stop=(k == 2 * g + 1),
                                  tokens=[hi_t[n], lo_t[n], *xs_t[k], *free[b]],
                                  done=(k == 2 * g + 1 and h == 1))
                done_t[g] = (b, t)

            product(0)
            product(1)
            t1 = token_sums(ssum, SB[:, 0, :], ss_t["t"])
            t2 = token_sums(ssum2, SB[:, 1, :], ss2["t"])
            product(2)
            product(3)
            used[n] = done_t[3][1]
            va, ra, ta = small[:, 4, 0:4], small[:, 5, 0:4], small[:, 6, 0:4]
            d = DV.do(lambda e: e.tensor_scalar(va[:, 0:2], SB[:, 0, 0:2], 1.0 / D, EPS, ALU.mult, ALU.add), t1)
            d2 = DV.do(lambda e: e.tensor_scalar(va[:, 2:4], SB[:, 1, 0:2], 1.0 / D, None, ALU.mult), t2)
            s_free["t"] = [d, d2]
            d = DV.do(lambda e: e.scalar_tensor_tensor(out=va[:, 2:4], in0=va[:, 0:2], scalar=EPS, in1=va[:, 2:4],
                                                       op0=ALU.mult, op1=ALU.add), d, d2)
            r_t["col"] = rsqrt(va, ra, ta, d)
            rms_row(ra, rb, 0)
            z_t = {}
            for g in range(NG):
                b, t = done_t[g]
                for h in range(2):
                    z_t[g] = AC.do(lambda e, g=g, h=h, b=b: e.activation(
                        zz[:, h, g * 256:(g + 1) * 256], bank[b][:, h * 256:(h + 1) * 256], ACT.Copy,
                        scale=ra[:, 2 + h:3 + h]), t, r_t["col"], PE.now())
                free[b] = [z_t[g]]
            t_win = (s_win, 16)
            for g in range(NG):
                b = take()
                for m in range(2):
                    ch_ = slice(g * 256 + m * 128, g * 256 + (m + 1) * 128)
                    PE.quiet(lambda e, g=g, m=m, b=b, ch_=ch_: e.matmul(
                        bank[b][:, m * 256:(m + 1) * 256], zz[:, 0, ch_], wins[:, g, 0:256], start=(m == 0),
                        stop=False, skip_group_check=True), z_t[g], t_win, *free[b])
                    t = PE.do(lambda e, g=g, m=m, b=b, ch_=ch_: e.matmul(
                        bank[b][:, m * 256 + 128:(m + 1) * 256], zz[:, 1, ch_], wins[:, g, 256:384], start=False,
                        stop=True, skip_group_check=True))
                done_t[g] = (b, t)
            row_t, x0_t = r_t["row"], {}
            rbb = rb[:, :].unsqueeze(1).to_broadcast([128, 2, S])
            for g in range(NG):
                E = DV if g < 2 else PO
                x0_t[g] = E.do(lambda e, g=g: e.tensor_tensor(xT[:, 2 * g:2 * g + 2, :], xT[:, 2 * g:2 * g + 2, :],
                                                              rbb, ALU.mult), row_t, *xs_t[2 * g],
                               *xs_t[2 * g + 1], ss_t["t"], ss2["t"])
            for k in range(KD):
                x_t[k] = DV.do(lambda e, k=k: e.tensor_scalar(xT[:, k, :], xT[:, k, :], vcol("norm_final", k),
                                                              bs[:, k:k + 1], ALU.mult, ALU.add), x0_t[k // 2])

            def join(g):
                b, t = done_t[g]
                for m, k in ((0, 2 * g), (1, 2 * g + 1)):
                    x_t[k] = DV.do(lambda e, k=k, m=m, b=b: e.scalar_tensor_tensor(
                        out=xT[:, k, :], in0=bank[b][:, m * 256:(m + 1) * 256], scalar=vcol("pool_scale", k),
                        in1=xT[:, k, :], op0=ALU.mult, op1=ALU.add), t, x_t[k])
                free[b] = [x_t[2 * g + 1]]

            for g in range(NG):
                join(g)
                lows = [split_x_hi(k, next_gain, next_gi + k) for k in (2 * g, 2 * g + 1)]
                add = squares(g, later=True)
                if g:
                    behind()
                behind = lambda lows=lows, add=add: [fn() for fn in (*lows, add)]
            behind()

        load_unit()
        SP.quiet(lambda e: e.dma_start(xT[:, 4:8, :], dram["x"][:, 4:8, :]).then_inc(s_x2, 16))
        load_unit()
        load_unit()
        SP.quiet(lambda e: e.dma_start(con[:, :], dram["con"]).then_inc(s_con, 16))
        for k in range(KD):
            x_t[k] = t_x if k < 4 else t_x2
        for k in range(4):
            split_x(k, "norm_mix", k)
        ready(0)
        for k in range(4, KD):
            split_x(k, "norm_mix", k)
        ready(1)
        for c in range(4):
            squares(c)
        heads_mixer(0, "norm_ffn", 0)
        ffn(0, ACT.Gelu, "norm_mix", 8)
        latent_mixer("norm_ffn", 8)
        pool_gains()
        ffn(1, ACT.Gelu, gg, 0, sums=2)
        pool_mixer("ffn_norm_2", 0)
        ffn(2, ACT.Silu, "mix_norm_2", 8)
        heads_mixer(3, "ffn_norm_2", 8)
        ffn(3, ACT.Silu, None, 0, sums=False)
        for c in range(4):
            SP.wait(x_t[2 * c])
            SP.quiet(lambda e, c=c: e.dma_start(out[:, 2 * c:2 * c + 2, :], xT[:, 2 * c:2 * c + 2, :]).then_inc(s_out,
                                                                                                               16))
        SP.quiet(lambda e: e.wait_ge(s_out, 64))

        block = ctx.enter_context(nc.Block())

        @block.sync
        def _(e):
            SP.play(e)

        @block.scalar
        def _(e):
            AC.play(e)

        @block.vector
        def _(e):
            DV.play(e)

        @block.gpsimd
        def _(e):
            PO.play(e)

        @block.tensor
        def _(e):
            PE.play(e)


def lay_units(w, cols, nk=None):
    k, n = w.shape
    v = w.reshape(k // 128, 128, n // cols, cols)
    return np.ascontiguousarray(v.transpose(2, 1, 0, 3)).reshape(n // cols, 128, k // 128 * cols)


def chan(v):
    return np.ascontiguousarray(v.reshape(-1, 128).T)


def constants():
    def rope(dim):
        inv = np.float32(10000.0) ** (-np.arange(0, dim, 2, dtype=np.float32) / np.float32(dim))
        ang = np.arange(S, dtype=np.float32)[:, None] * inv[None, :].astype(np.float32)
        c, s = np.cos(ang).astype(np.float32), np.sin(ang).astype(np.float32)
        lay = lambda a: a.reshape(2, 128, dim).transpose(1, 0, 2).reshape(128, 2 * dim)
        return lay(np.concatenate([c, c], 1)), lay(np.concatenate([-s, s], 1))

    p = np.arange(128)[:, None]
    c0, s0 = rope(64)
    c1, s1 = rope(32)
    k0, k1 = np.arange(128)[None, :], np.arange(256)[None, :]
    big = np.float32(-1e30)
    mask0 = np.concatenate([np.where(k0 <= p, 0, big), np.where(k1 <= p + 128, 0, big)], 1)
    mask3 = np.concatenate([np.where(k0 // 64 <= p // 64, 0, big),
                            np.where(k1 // 64 <= (p + 128) // 64, 0, big)], 1)
    return np.ascontiguousarray(np.concatenate([np.eye(128), c0, s0, c1, s1, mask0, mask3], 1),
                                dtype=np.float32)


def windows():
    src, dst = np.arange(S)[:, None], np.arange(S)[None, :]
    both = []
    for w in (2, 4, 8, 16):
        a = np.where((src <= dst) & (src > dst - w), 1.0 / np.minimum(dst + 1, w), 0.0) - np.eye(S)
        both.append(np.concatenate([a[0:128], a[128:256, 128:256]], 1))
    return np.ascontiguousarray(np.stack(both, 1), dtype=np.float32)


def kernel(**inputs):
    import concourse.bacc as _bacc
    from concourse.bass_utils import run_bass_kernel_spmd as _run

    i = {k: np.asarray(v) for k, v in inputs.items()}
    a = {}
    a["x"] = i["x"][0].T.reshape(KD, 128, S).transpose(1, 0, 2)
    a["con"] = constants()
    a["win"] = windows()
    a["vec"] = np.concatenate([
        chan(i["norm_mix"]), chan(i["norm_ffn"]), chan(i["norm_final"]), chan(i["mix_norm_2"]),
        chan(i["ffn_norm_2"]), chan(i["pool_b_2"]), chan(i["pool_scale_2"]), chan(i["b_q_norm"]),
        chan(i["b_kv_norm"]), chan(np.concatenate([i["attn_q_norm_2"], i["attn_q_norm_2"]], 1)),
        chan(np.concatenate([i["attn_k_norm_2"], i["attn_k_norm_2"]], 1)),
        chan(i["ffn_conv_w"]), chan(i["ffn_conv_w_2"]), chan(i["ffn_conv_b"]), chan(i["ffn_conv_b_2"])], 1)
    a["a_qkv"] = lay_units(i["a_w_qkv"][0], 256)
    a["a_o"] = lay_units(i["a_w_o"][0], 256)
    a["b_in"] = lay_units(i["b_w_in"][0][:, 0:512], 256)
    a["b_in2"] = lay_units(i["b_w_in"][0][:, 512:672], 160)
    a["b_uq"] = lay_units(i["b_w_uq"][0], 384)
    a["b_ukv"] = lay_units(i["b_w_ukv"][0], 512)
    a["b_o"] = lay_units(i["b_w_o"][0], 256)
    a["pool"] = i["pool_w_2"][0].reshape(8, 128, 256).transpose(1, 0, 2).reshape(1, 128, 2048)
    a["d_qkv"] = lay_units(i["attn_wqkv_2"][0], 256)
    a["d_o"] = lay_units(i["attn_wo_2"][0], 256)
    for layer in range(4):
        j = layer % 2
        g, u, d = (("ffn_w_gate", "ffn_w_up", "ffn_w_down"), ("ffn_w_gate_2", "ffn_w_val_2", "ffn_w_out_2"))[
            layer // 2]
        a[f"gate{layer}"] = lay_units(i[g][j], 256)
        a[f"up{layer}"] = lay_units(i[u][j], 256)
        for c, (k0, k1) in enumerate(((0, 1024), (1024, 2048), (2048, 2816))):
            a[f"down{layer}_{c}"] = lay_units(i[d][j][k0:k1], 256)
    idx = 384 + np.arange(128)[:, None] - np.arange(256)[None, :]
    a["bias"] = i["attn_rel_bias_2"][0][:, idx].reshape(4, 4, 128, 256).transpose(0, 2, 1, 3)
    a = {k: np.ascontiguousarray(v, dtype=v.dtype) for k, v in a.items()}

    nc = _bacc.Bacc("TRN2", target_bir_lowering=False, num_devices=1, dynamic_dma_scratch_size=1024)
    dram = {k: nc.dram_tensor(f"in_{k}", v.shape, mybir.dt.from_np(v.dtype), kind="ExternalInput").ap()
            for k, v in a.items()}
    out = nc.dram_tensor("out_0", (128, KD, S), F32, kind="ExternalOutput").ap()
    build(nc, dram, out)
    r = _run(nc, [{f"in_{k}": v for k, v in a.items()}], core_ids=[0])
    got = r.results[0]["out_0"]
    return np.ascontiguousarray(got.transpose(1, 0, 2).reshape(D, S).T).reshape(1, S, D)
```
